# Optimizing a Trainium2 kernel written in Bass

```python
import math
import jax, jax.numpy as jnp
from jax import lax
import numpy as np

D_MODEL = 1024
BATCH = 1
SEQ = 512
DEPTH = 1

D_RNN = 1024
N_RNN_BLOCKS = 8
RNN_BLOCK = D_RNN // N_RNN_BLOCKS
CONV_WIDTH = 4
LRU_C = 8.0
HEAD_DIM = 64
N_Q_HEADS = 16
N_KV_HEADS = 4
Q_PER_KV = N_Q_HEADS // N_KV_HEADS
D_ATTN = N_Q_HEADS * HEAD_DIM
D_KV = N_KV_HEADS * HEAD_DIM
WINDOW = 128
BLOCK = 128
ROPE_DIM = HEAD_DIM // 4
ROPE_THETA = 500000.0
NORM_EPS = 1e-6

OFF_RNN_X = 0
OFF_RNN_G = OFF_RNN_X + D_RNN
OFF_Q = OFF_RNN_G + D_RNN
OFF_K = OFF_Q + D_ATTN
OFF_V = OFF_K + D_KV
OFF_ATTN_G = OFF_V + D_KV
OFF_MERGE_R = OFF_ATTN_G + D_ATTN
OFF_MERGE_A = OFF_MERGE_R + D_MODEL
D_IN = OFF_MERGE_A + D_MODEL


def rms_norm(x, g):
    xf = x.astype(jnp.float32)
    y = xf * lax.rsqrt(jnp.mean(xf * xf, axis=-1, keepdims=True) + NORM_EPS)
    return (y * g.astype(jnp.float32)).astype(x.dtype)

def causal_depthwise_conv(u, w, b):
    C = u.shape[-1]
    y = lax.conv_general_dilated(
        u, w.astype(u.dtype)[:, None, :], window_strides=(1,),
        padding=[(CONV_WIDTH - 1, 0)], dimension_numbers=("NWC", "WIO", "NWC"),
        feature_group_count=C)
    return y + b.astype(u.dtype)

def block_diag_linear(u, w, b):
    B, S, _ = u.shape
    ub = u.reshape(B, S, N_RNN_BLOCKS, RNN_BLOCK)
    y = jnp.einsum("bsnc,ncd->bsnd", ub, w.astype(u.dtype))
    return y.reshape(B, S, D_RNN) + b.astype(u.dtype)

def rg_lru(u, w_a, b_a, w_x, b_x, lam):
    r = jax.nn.sigmoid(block_diag_linear(u, w_a, b_a).astype(jnp.float32))
    i = jax.nn.sigmoid(block_diag_linear(u, w_x, b_x).astype(jnp.float32))
    log_a = -LRU_C * r * jax.nn.softplus(-lam.astype(jnp.float32))
    a = jnp.exp(log_a)
    b = jnp.sqrt(-jnp.expm1(2.0 * log_a)) * (i * u.astype(jnp.float32))

    def combine(c1, c2):
        a1, b1 = c1
        a2, b2 = c2
        return a1 * a2, a2 * b1 + b2

    _, h = lax.associative_scan(combine, (a, b), axis=1)
    return h.astype(u.dtype)

def rope_tables(seq_len):
    pos = jnp.arange(seq_len, dtype=jnp.float32)
    inv_freq = ROPE_THETA ** (-jnp.arange(0, ROPE_DIM, 2, dtype=jnp.float32) / ROPE_DIM)
    ang = pos[:, None] * inv_freq[None, :]
    return jnp.cos(ang)[:, None, :], jnp.sin(ang)[:, None, :]

def apply_partial_rope(t, cos, sin):
    half = ROPE_DIM // 2
    c = cos.astype(t.dtype)
    s = sin.astype(t.dtype)
    t1 = t[..., :half]
    t2 = t[..., half:ROPE_DIM]
    rot = jnp.concatenate([t1 * c - t2 * s, t2 * c + t1 * s], axis=-1)
    return jnp.concatenate([rot, t[..., ROPE_DIM:]], axis=-1)

def sliding_window_attention_with_sinks(q, k, v, sinks):
    B, S, _, _ = q.shape
    nb = S // BLOCK
    qb = q.reshape(B, nb, BLOCK, N_KV_HEADS, Q_PER_KV, HEAD_DIM)
    kb = k.reshape(B, nb, BLOCK, N_KV_HEADS, HEAD_DIM)
    vb = v.reshape(B, nb, BLOCK, N_KV_HEADS, HEAD_DIM)
    zeros = jnp.zeros_like(kb[:, :1])
    kw = jnp.concatenate([jnp.concatenate([zeros, kb[:, :-1]], axis=1), kb], axis=2)
    vw = jnp.concatenate([jnp.concatenate([zeros, vb[:, :-1]], axis=1), vb], axis=2)

    scale = 1.0 / math.sqrt(HEAD_DIM)
    scores = jnp.einsum("bnqkgd,bnjkd->bnkgqj", qb, kw).astype(jnp.float32) * scale

    blk = jnp.arange(nb)[:, None, None]
    q_abs = blk * BLOCK + jnp.arange(BLOCK)[None, :, None]
    k_abs = (blk - 1) * BLOCK + jnp.arange(2 * BLOCK)[None, None, :]
    valid = (k_abs <= q_abs) & (q_abs - k_abs < WINDOW) & (k_abs >= 0)
    scores = jnp.where(valid[None, :, None, None, :, :], scores, -jnp.inf)

    sink = sinks.astype(jnp.float32).reshape(N_KV_HEADS, Q_PER_KV)[None, None, :, :, None]
    m = jnp.maximum(jnp.max(scores, axis=-1), sink)
    p = jnp.exp(scores - m[..., None])
    denom = jnp.sum(p, axis=-1) + jnp.exp(sink - m)
    probs = (p / denom[..., None]).astype(v.dtype)
    out = jnp.einsum("bnkgqj,bnjkd->bnqkgd", probs, vw)
    return out.reshape(B, S, D_ATTN)

def first_inputs(seed: int = 0) -> dict:
    key = jax.random.key(seed)
    ks = jax.random.split(key, 17)
    f32 = jnp.float32
    x = jax.random.normal(ks[0], (BATCH, SEQ, D_MODEL), f32)
    norm_g = 1.0 + 0.02 * jax.random.normal(ks[1], (DEPTH, D_MODEL), f32)
    w_in = jax.random.normal(ks[2], (DEPTH, D_MODEL, D_IN), f32) * D_MODEL ** -0.5
    conv_w = jax.random.normal(ks[3], (DEPTH, CONV_WIDTH, D_RNN), f32) * CONV_WIDTH ** -0.5
    conv_b = 0.02 * jax.random.normal(ks[4], (DEPTH, D_RNN), f32)
    lru_w_a = jax.random.normal(ks[5], (DEPTH, N_RNN_BLOCKS, RNN_BLOCK, RNN_BLOCK), f32) * RNN_BLOCK ** -0.5
    lru_b_a = 0.02 * jax.random.normal(ks[6], (DEPTH, D_RNN), f32)
    lru_w_x = jax.random.normal(ks[7], (DEPTH, N_RNN_BLOCKS, RNN_BLOCK, RNN_BLOCK), f32) * RNN_BLOCK ** -0.5
    lru_b_x = 0.02 * jax.random.normal(ks[8], (DEPTH, D_RNN), f32)
    a0 = jax.random.uniform(ks[9], (DEPTH, D_RNN), f32, 0.9, 0.999)
    lru_lambda = jnp.log(a0) - jnp.log1p(-a0)
    attn_sinks = 0.5 * jax.random.normal(ks[10], (DEPTH, N_Q_HEADS), f32)
    w_rnn_out = jax.random.normal(ks[11], (DEPTH, D_RNN, D_MODEL), f32) * D_RNN ** -0.5
    w_attn_out = jax.random.normal(ks[12], (DEPTH, D_ATTN, D_MODEL), f32) * D_ATTN ** -0.5
    w_o = jax.random.normal(ks[13], (DEPTH, D_MODEL, D_MODEL), f32) * D_MODEL ** -0.5
    final_norm_g = 1.0 + 0.02 * jax.random.normal(ks[14], (D_MODEL,), f32)
    return {"x": x, "norm_g": norm_g, "w_in": w_in, "conv_w": conv_w, "conv_b": conv_b,
            "lru_w_a": lru_w_a, "lru_b_a": lru_b_a, "lru_w_x": lru_w_x, "lru_b_x": lru_b_x,
            "lru_lambda": lru_lambda, "attn_sinks": attn_sinks, "w_rnn_out": w_rnn_out,
            "w_attn_out": w_attn_out, "w_o": w_o, "final_norm_g": final_norm_g}

def first_block(x, norm_g, w_in, conv_w, conv_b, lru_w_a, lru_b_a, lru_w_x, lru_b_x,
              lru_lambda, attn_sinks, w_rnn_out, w_attn_out, w_o, final_norm_g):
    B, S, _ = x.shape
    cos, sin = rope_tables(S)
    for l in range(DEPTH):
        h = rms_norm(x, norm_g[l])
        proj = jnp.einsum("bsd,de->bse", h, w_in[l])
        u = proj[..., OFF_RNN_X:OFF_RNN_G]
        g_rnn = proj[..., OFF_RNN_G:OFF_Q]
        q = proj[..., OFF_Q:OFF_K].reshape(B, S, N_Q_HEADS, HEAD_DIM)
        k = proj[..., OFF_K:OFF_V].reshape(B, S, N_KV_HEADS, HEAD_DIM)
        v = proj[..., OFF_V:OFF_ATTN_G].reshape(B, S, N_KV_HEADS, HEAD_DIM)
        g_attn = proj[..., OFF_ATTN_G:OFF_MERGE_R]
        m_rnn = proj[..., OFF_MERGE_R:OFF_MERGE_A]
        m_attn = proj[..., OFF_MERGE_A:D_IN]

        u = causal_depthwise_conv(u, conv_w[l], conv_b[l])
        y_rnn = rg_lru(u, lru_w_a[l], lru_b_a[l], lru_w_x[l], lru_b_x[l], lru_lambda[l]) * jax.nn.silu(g_rnn)

        q = apply_partial_rope(q, cos, sin)
        k = apply_partial_rope(k, cos, sin)
        y_attn = sliding_window_attention_with_sinks(q, k, v, attn_sinks[l]) * jax.nn.silu(g_attn)

        merged = (jax.nn.sigmoid(m_rnn) * jnp.einsum("bsr,rd->bsd", y_rnn, w_rnn_out[l])
                  + jax.nn.sigmoid(m_attn) * jnp.einsum("bsa,ad->bsd", y_attn, w_attn_out[l]))
        x = x + jnp.einsum("bsd,de->bse", merged, w_o[l])
    return rms_norm(x, final_norm_g)


DEPTH_2 = 2

N_MIXERS = 2
N_HEADS = 16
GROUP = N_HEADS // N_KV_HEADS
IDX_HEADS = 8
IDX_DIM = 64
TOPK_MAX = 256
Q_BLOCK = 128
ROPE_THETA_2 = 10000.0
CONV_WIDTH_2 = 3
FFN_HIDDEN = int(math.ceil(8 * D_MODEL / 3 / 256) * 256)
N_A = (DEPTH_2 + 1) // 2
N_B = DEPTH_2 // 2

Q_COLS = N_HEADS * HEAD_DIM
K_COLS = N_KV_HEADS * HEAD_DIM
V_COLS = N_KV_HEADS * HEAD_DIM
QI_COLS = IDX_HEADS * IDX_DIM
KI_COLS = IDX_DIM
WI_COLS = IDX_HEADS
ATTN_IN_COLS = Q_COLS + K_COLS + V_COLS + QI_COLS + KI_COLS + WI_COLS


def _rmsnorm(x, g):
    xf = x.astype(jnp.float32)
    y = xf * lax.rsqrt(jnp.mean(xf * xf, axis=-1, keepdims=True) + NORM_EPS)
    return (y * g.astype(jnp.float32)).astype(x.dtype)

def _layernorm(x, g, b):
    xf = x.astype(jnp.float32)
    mu = jnp.mean(xf, axis=-1, keepdims=True)
    var = jnp.mean(jnp.square(xf - mu), axis=-1, keepdims=True)
    y = (xf - mu) * lax.rsqrt(var + NORM_EPS)
    return (y * g.astype(jnp.float32) + b.astype(jnp.float32)).astype(x.dtype)

def _rope(x, pos):
    d = x.shape[-1]
    half = d // 2
    inv_freq = ROPE_THETA_2 ** (-(jnp.arange(half, dtype=jnp.float32) * 2.0 / d))
    ang = pos.astype(jnp.float32)[..., None] * inv_freq
    cos = jnp.cos(ang)[:, :, None, :]
    sin = jnp.sin(ang)[:, :, None, :]
    xf = x.astype(jnp.float32)
    x1, x2 = xf[..., :half], xf[..., half:]
    out = jnp.concatenate([x1 * cos - x2 * sin, x2 * cos + x1 * sin], axis=-1)
    return out.astype(x.dtype)

def _dsa_mixer(h, positions, w_in, q_norm_g, k_norm_g, idx_k_ln_g, idx_k_ln_b, w_out):
    Bn, T, _ = h.shape
    proj = h @ w_in
    o0 = 0
    q = proj[..., o0:o0 + Q_COLS].reshape(Bn, T, N_HEADS, HEAD_DIM); o0 += Q_COLS
    k = proj[..., o0:o0 + K_COLS].reshape(Bn, T, N_KV_HEADS, HEAD_DIM); o0 += K_COLS
    v = proj[..., o0:o0 + V_COLS].reshape(Bn, T, N_KV_HEADS, HEAD_DIM); o0 += V_COLS
    qi = proj[..., o0:o0 + QI_COLS].reshape(Bn, T, IDX_HEADS, IDX_DIM); o0 += QI_COLS
    ki = proj[..., o0:o0 + KI_COLS]; o0 += KI_COLS
    wi = proj[..., o0:o0 + WI_COLS]

    q = _rope(_rmsnorm(q, q_norm_g), positions)
    k = _rope(_rmsnorm(k, k_norm_g), positions)
    qi = _rope(qi, positions)
    ki = _rope(_layernorm(ki, idx_k_ln_g, idx_k_ln_b)[:, :, None, :], positions)[:, :, 0, :]
    wi = wi * (IDX_HEADS ** -0.5 * IDX_DIM ** -0.5)

    topk = min(TOPK_MAX, T // 4)
    n_blk = T // Q_BLOCK
    key_idx = jnp.arange(T)
    scale = HEAD_DIM ** -0.5

    def to_blocks(a):
        return jnp.moveaxis(a.reshape(Bn, n_blk, Q_BLOCK, *a.shape[2:]), 1, 0)

    def block_fn(args):
        qb, qib, wib, start = args
        t_idx = start + jnp.arange(Q_BLOCK)
        s = jnp.einsum('bqhd,bsd->bqhs', qib, ki)
        score = jnp.einsum('bqhs,bqh->bqs', jax.nn.relu(s), wib).astype(jnp.float32)
        causal = key_idx[None, :] <= t_idx[:, None]
        score = jnp.where(causal[None], score, -jnp.inf)
        _, sel = lax.top_k(score, topk)
        sel_ok = sel <= t_idx[None, :, None]
        kg = jax.vmap(lambda a, i: a[i])(k, sel)
        vg = jax.vmap(lambda a, i: a[i])(v, sel)
        qg = qb.reshape(Bn, Q_BLOCK, N_KV_HEADS, GROUP, HEAD_DIM)
        logits = jnp.einsum('bqgrd,bqkgd->bqgrk', qg, kg).astype(jnp.float32) * scale
        logits = jnp.where(sel_ok[:, :, None, None, :], logits, -1e30)
        p = jax.nn.softmax(logits, axis=-1).astype(vg.dtype)
        o = jnp.einsum('bqgrk,bqkgd->bqgrd', p, vg)
        return o.reshape(Bn, Q_BLOCK, N_HEADS * HEAD_DIM)

    starts = jnp.arange(n_blk) * Q_BLOCK
    o = lax.map(block_fn, (to_blocks(q), to_blocks(qi), to_blocks(wi), starts))
    o = jnp.moveaxis(o, 0, 1).reshape(Bn, T, N_HEADS * HEAD_DIM)
    return o @ w_out

def _short_conv_mixer(h, w_in, conv_w, w_out):
    proj = h @ w_in
    b_gate, c_gate, u = jnp.split(proj, 3, axis=-1)
    z = c_gate * u
    z = lax.conv_general_dilated(
        z, conv_w[:, None, :].astype(z.dtype),
        window_strides=(1,), padding=[(CONV_WIDTH_2 - 1, 0)],
        dimension_numbers=('NWC', 'WIO', 'NWC'),
        feature_group_count=z.shape[-1])
    return (b_gate * z) @ w_out

def _swiglu(h, w_gate, w_up, w_down):
    return (jax.nn.silu(h @ w_gate) * (h @ w_up)) @ w_down

def second_inputs(seed: int = 0) -> dict:
    key = jax.random.key(seed)
    ks = jax.random.split(key, 20)
    D = D_MODEL

    def nrm(k, shape, s):
        return jax.random.normal(k, shape, dtype=jnp.float32) * s

    x = nrm(ks[0], (BATCH, SEQ, D), 1.0)
    c = nrm(ks[1], (BATCH, D), 1.0)
    positions = (jnp.arange(SEQ, dtype=jnp.int32)[None, :]
                 + jax.random.randint(ks[2], (BATCH, 1), 0, 1024, dtype=jnp.int32))
    ada_w = nrm(ks[3], (DEPTH_2, D, 6 * D), 0.5 * D ** -0.5)
    ada_b = nrm(ks[4], (DEPTH_2, 6 * D), 0.02)
    norm1_g = 1.0 + nrm(ks[5], (DEPTH_2, D), 0.02)
    norm2_g = 1.0 + nrm(ks[6], (DEPTH_2, D), 0.02)
    attn_w_in = nrm(ks[7], (N_A, D, ATTN_IN_COLS), D ** -0.5)
    attn_q_norm_g = 1.0 + nrm(ks[8], (N_A, HEAD_DIM), 0.02)
    attn_k_norm_g = 1.0 + nrm(ks[9], (N_A, HEAD_DIM), 0.02)
    idx_k_ln_g = 1.0 + nrm(ks[10], (N_A, IDX_DIM), 0.02)
    idx_k_ln_b = nrm(ks[11], (N_A, IDX_DIM), 0.02)
    attn_w_out = nrm(ks[12], (N_A, N_HEADS * HEAD_DIM, D), (N_HEADS * HEAD_DIM) ** -0.5)
    conv_w_in = nrm(ks[13], (N_B, D, 3 * D), D ** -0.5)
    conv_w = nrm(ks[14], (N_B, CONV_WIDTH_2, D), CONV_WIDTH_2 ** -0.5)
    conv_w_out = nrm(ks[15], (N_B, D, D), D ** -0.5)
    ffn_w_gate = nrm(ks[16], (DEPTH_2, D, FFN_HIDDEN), D ** -0.5)
    ffn_w_up = nrm(ks[17], (DEPTH_2, D, FFN_HIDDEN), D ** -0.5)
    ffn_w_down = nrm(ks[18], (DEPTH_2, FFN_HIDDEN, D), FFN_HIDDEN ** -0.5)
    return {"x": x, "c": c, "positions": positions,
            "ada_w": ada_w, "ada_b": ada_b, "norm1_g": norm1_g, "norm2_g": norm2_g,
            "attn_w_in": attn_w_in, "attn_q_norm_g": attn_q_norm_g,
            "attn_k_norm_g": attn_k_norm_g, "idx_k_ln_g": idx_k_ln_g,
            "idx_k_ln_b": idx_k_ln_b, "attn_w_out": attn_w_out,
            "conv_w_in": conv_w_in, "conv_w": conv_w, "conv_w_out": conv_w_out,
            "ffn_w_gate": ffn_w_gate, "ffn_w_up": ffn_w_up, "ffn_w_down": ffn_w_down}

def second_block(x, c, positions, ada_w, ada_b, norm1_g, norm2_g,
              attn_w_in, attn_q_norm_g, attn_k_norm_g, idx_k_ln_g, idx_k_ln_b, attn_w_out,
              conv_w_in, conv_w, conv_w_out, ffn_w_gate, ffn_w_up, ffn_w_down):
    c_act = jax.nn.silu(c)
    for i in range(DEPTH_2):
        mod = c_act @ ada_w[i] + ada_b[i]
        sh1, sc1, g1, sh2, sc2, g2 = [m[:, None, :] for m in jnp.split(mod, 6, axis=-1)]
        h = _rmsnorm(x, norm1_g[i]) * (1.0 + sc1) + sh1
        if i % N_MIXERS == 0:
            j = i // N_MIXERS
            y = _dsa_mixer(h, positions, attn_w_in[j], attn_q_norm_g[j], attn_k_norm_g[j],
                           idx_k_ln_g[j], idx_k_ln_b[j], attn_w_out[j])
        else:
            j = i // N_MIXERS
            y = _short_conv_mixer(h, conv_w_in[j], conv_w[j], conv_w_out[j])
        x = x + g1 * y
        h = _rmsnorm(x, norm2_g[i]) * (1.0 + sc2) + sh2
        x = x + g2 * _swiglu(h, ffn_w_gate[i], ffn_w_up[i], ffn_w_down[i])
    return x


def setup_inputs(seed=0):
    out = dict(first_inputs(seed))
    for name, value in second_inputs(seed + 1).items():
        if name != "x":
            out[name + "_2"] = value
    return out


def reference(
    x, norm_g, w_in, conv_w, conv_b, lru_w_a, lru_b_a, lru_w_x, lru_b_x, lru_lambda, attn_sinks,
    w_rnn_out, w_attn_out, w_o, final_norm_g, c_2, positions_2, ada_w_2, ada_b_2, norm1_g_2,
    norm2_g_2, attn_w_in_2, attn_q_norm_g_2, attn_k_norm_g_2, idx_k_ln_g_2, idx_k_ln_b_2,
    attn_w_out_2, conv_w_in_2, conv_w_2, conv_w_out_2, ffn_w_gate_2, ffn_w_up_2, ffn_w_down_2,
):
    x = first_block(
        x, norm_g, w_in, conv_w, conv_b, lru_w_a, lru_b_a, lru_w_x, lru_b_x, lru_lambda,
        attn_sinks, w_rnn_out, w_attn_out, w_o, final_norm_g,
    )
    return second_block(
        x, c_2, positions_2, ada_w_2, ada_b_2, norm1_g_2, norm2_g_2, attn_w_in_2,
        attn_q_norm_g_2, attn_k_norm_g_2, idx_k_ln_g_2, idx_k_ln_b_2, attn_w_out_2, conv_w_in_2,
        conv_w_2, conv_w_out_2, ffn_w_gate_2, ffn_w_up_2, ffn_w_down_2,
    )


_drawn_inputs = setup_inputs


def setup_inputs(seed=0):
    import zlib

    import numpy as np

    out = dict(_drawn_inputs(seed))
    spreads = {}
    factors = {'norm_g': 7.012,
     'conv_b': 3.225,
     'lru_b_a': 8.0,
     'lru_b_x': 8.0,
     'attn_sinks': 8.0,
     'norm1_g_2': 4.044,
     'norm2_g_2': 6.439,
     'attn_q_norm_g_2': 8.0,
     'attn_k_norm_g_2': 8.0,
     'idx_k_ln_g_2': 8.0,
     'idx_k_ln_b_2': 8.0}
    for name, (base, spread) in spreads.items():
        noise = np.random.default_rng([zlib.crc32(name.encode()), seed]).standard_normal(out[name].shape)
        drawn = base * np.exp(spread * noise) if base else spread * noise
        out[name] = __import__('jax').numpy.asarray(drawn.astype(out[name].dtype))
    for name, factor in factors.items():
        out[name] = (out[name] * factor).astype(out[name].dtype)
    return out
```

```python
from contextlib import ExitStack, contextmanager
import math

import numpy as np

import concourse.bass as bass
from concourse import mybir

F32 = mybir.dt.float32
F32R = mybir.dt.float32r
I32 = mybir.dt.int32
ACT = mybir.ActivationFunctionType
ALU = mybir.AluOpType
AXX = mybir.AxisListType.X

P = 128
S = 512
KC = 8
NB = S // P
BIG = KC * S
HD = 64
NKV = 4
TILE = KC * P
HALF = TILE // 2
FFN_CHUNKS = 22
FFN_GROUPS = [8, 8, 6]
EPS = 1e-6
SCALE = HD ** -0.5
NEG = -1e30
TAKEN = -3e38
TOPK = 128


CST = {}
_at = 0
for _name, _n in (("ident", P), ("rot1", P), ("rot2", P), ("mean_head", P), ("sel_all", 1), ("sel_head", 2),
                  ("mask_prev", P), ("mask_diag", P), ("sin_sign", 1), ("inv_freq", 1)):
    CST[_name] = (_at, _n)
    _at += _n
CST_COLS = _at

PRM = {}
_at = 0
for _name, _n in (("norm_g", 8), ("final_g", 8), ("conv_w", 32), ("conv_b", 8), ("b_a", 8), ("b_x", 8),
                  ("lam", 8), ("sinks", 16), ("norm1_g", 16), ("norm2_g", 16), ("ada_b", 96), ("c", 8),
                  ("q_g", 1), ("k_g", 1), ("ki_g", 1), ("ki_b", 1), ("conv3_w", 24)):
    PRM[_name] = (_at, _n)
    _at += _n
PRM_COLS = _at


def constant_columns():
    out = np.zeros((P, CST_COLS), np.float32)

    def put(name, a):
        at, n = CST[name]
        out[:, at:at + n] = a

    put("ident", np.eye(P))
    for name, half, width in (("rot1", 8, 16), ("rot2", 32, 64)):
        rot = np.zeros((P, P), np.float32)
        for head in (0, HD):
            for i in range(width):
                rot[head + (i + half) % width, head + i] = 1.0
        put(name, rot)
    put("sel_all", np.full((P, 1), 1.0 / (KC * P)))
    put("sel_head", np.kron(np.eye(2), np.full((HD, 1), 1.0 / HD)))
    put("mean_head", np.kron(np.eye(2), np.full((HD, HD), 1.0 / HD)))
    q, k = np.arange(P)[:, None], np.arange(P)[None, :]
    put("mask_prev", np.where(k > q, 0.0, NEG))
    put("mask_diag", np.where(k <= q, 0.0, NEG))
    d = np.arange(P) % HD
    put("sin_sign", np.where(d < 32, -1.0, 1.0)[:, None])
    put("inv_freq", (10000.0 ** (-((d % 32) * 2.0 / HD))).astype(np.float32)[:, None])
    return out


def first_rope_tables():
    half = 8
    freq = (500000.0 ** (-np.arange(0, 2 * half, 2, dtype=np.float64) / (2 * half))).astype(np.float32)
    ang = (np.arange(S, dtype=np.float32)[:, None] * freq[None, :]).astype(np.float64)
    cos, sin = np.ones((P, S), np.float32), np.zeros((P, S), np.float32)
    for head in (0, HD):
        cos[head:head + 2 * half] = np.concatenate([np.cos(ang), np.cos(ang)], 1).T
        sin[head:head + 2 * half] = np.concatenate([-np.sin(ang), np.sin(ang)], 1).T
    return np.concatenate([cos, sin], 1)


def stream_plan():
    plan = [("w_in", e) for e in range(8)]
    plan += [("w_in", 16 + e) for e in range(8)]
    plan += [("w_in", 24 + e) for e in range(4)]
    ga, gr, mr = 28, 8, 36
    plan += [("w_in", ga), ("w_in", ga + 1)]
    for pair in FILL:
        for kind, j in pair:
            plan.append({"ga": ("w_in", ga + j), "gr": ("w_in", gr + j), "mr": ("w_in", mr + j),
                         "R": ("w_rnn_out", j)}[kind])
    for j in range(8):
        plan += [("w_in", 44 + j), ("w_attn_out", j)]
    plan += [("w_o", e) for e in range(8)]

    def ffn(layer):
        out, g0 = [], 0
        groups = []
        for n in FFN_GROUPS:
            groups.append([(w + str(layer), j) for j in range(g0, g0 + n) for w in ("gate", "up")])
            g0 += n
        downs = [[("down" + str(layer), e, g) for e in range(8)] for g in range(3)]
        for part in (groups[0], groups[1], downs[0], groups[2], downs[1], downs[2]):
            out += part
        return out

    plan += [("attn_in", e) for e in range(17)]
    plan += [("attn_out", e) for e in range(8)]
    plan += ffn(0)
    for j in range(8):
        plan += [("conv_in", 8 + j), ("conv_in", 16 + j)]
    plan += [("conv_in", j) for j in range(8)]
    plan += [("conv_out", e) for e in range(8)]
    plan += ffn(1)
    return plan


FILL = [[("gr", 0), ("gr", 1)], [("gr", 2), ("gr", 3)], [("ga", 2), ("ga", 3)], [("gr", 4), ("gr", 5)],
        [("gr", 6), ("gr", 7)], [("ga", 4), ("ga", 5)], [("ga", 6), ("ga", 7)]] + \
       [[("mr", j), ("R", j)] for j in range(8)]

T_U, T_Q, T_K, T_V, T_GA, T_FILL = 0, 8, 16, 18, 20, 22
T_MA = T_FILL + 2 * len(FILL)
T_WO = T_MA + 16
T_QKV2 = T_WO + 8
T_AO2 = T_QKV2 + 17
T_FFN0 = T_AO2 + 8
T_CONV = T_FFN0 + 2 * FFN_CHUNKS + 24
T_CONVB = T_CONV + 16
T_CO = T_CONVB + 8
T_FFN1 = T_CO + 8
T_END = T_FFN1 + 2 * FFN_CHUNKS + 24

ADA_W = 512
ADA_RANGES = 6 * KC * P // ADA_W
ADA_COUNT = (3, 3, 2, 0)


class Tile:

    def __init__(self, t0, i=0):
        self.t0, self.i = t0, i
        self.n = i * 4 + t0
        self.slot = t0 % 4
        self.turn = i + t0 // 4
        self.bank = t0 % 2
        self.uses = i * 2 + t0 // 2

    def next(self):
        return Tile(self.t0 + 1, self.i)


class Tally:

    def __init__(self, sem):
        self.sem, self.n = sem, 0

    def up(self, instruction, by=1):
        instruction.then_inc(self.sem, by)
        self.n = self.n + by
        return instruction


@contextmanager
def looped(eng, count, tally=None, per=0):
    base = tally.n if tally else 0
    with eng.Fori(0, count) as i:
        if tally:
            tally.n = i * per + base
        yield i
    if tally:
        tally.n = base + per * count


def ds(at, n):
    return slice(at, at + n) if isinstance(at, int) else bass.ds(at, n)


def att_steps(block):
    if block == 1:
        return [(g, n, [n] if n == 0 else [n - 1, n]) for g in range(NKV) for n in range(NB)]
    return [(g, n, list(range(n + 1))) for n in range(NB) for g in range(NKV)]


def build(nc, x, stream, ada, lru_w, prm, cst, rope1, pos, out):
    with ExitStack() as ctx:
        base = (nc.sbuf_base + 31) // 32 * 32
        cursor = [base]

        def at(name, cols, where=None, dt=F32):
            if where is None:
                where = cursor[0]
                cursor[0] += (cols * 4 + 31) // 32 * 32
            return nc.alloc_sbuf_tensor_at(name, [P, cols], dt, offset=where)

        unit = [base + k * BIG * 4 for k in range(8)]
        cursor[0] = base + 8 * BIG * 4
        X = at("X", BIG, unit[0])
        H_hi = at("H_hi", BIG, unit[1], F32R)
        H_lo = at("H_lo", BIG, unit[2], F32R)
        U = at("U", BIG, unit[3])
        MG = at("MG", BIG, unit[3])
        MG_hi = at("MG_hi", BIG, unit[3], F32R)
        R = at("R", BIG, unit[4])
        YR_hi = at("YR_hi", BIG, unit[4], F32R)
        MG_lo = at("MG_lo", BIG, unit[4], F32R)
        Q = at("Q", BIG, unit[5])
        YA_hi = at("YA_hi", BIG, unit[5], F32R)
        I = at("I", BIG, unit[6])
        YR_lo = at("YR_lo", BIG, unit[6], F32R)
        LW = at("LW", 2 * KC * P, unit[7])
        T = at("T", BIG, unit[7])
        GA = at("GA", BIG, unit[7])
        YA_lo = at("YA_lo", BIG, unit[7], F32R)
        QI = at("QI", 4 * S, unit[3])
        BIAS = at("BIAS", 4 * S, unit[3] + BIG * 2)
        SB2 = at("SB2", 2 * 4 * S, unit[4])
        PT2 = at("PT2", 4 * S, unit[6])
        WORK = at("WORK", S, unit[6] + BIG * 2)
        RL = at("RL", 2 * S, unit[6] + BIG * 2 + S * 4)
        SCALL = at("SCALL", 3 * S, unit[2])
        YA2_lo = at("YA2_lo", BIG, unit[1], F32R)
        A_hi = [at("A0_hi", BIG, unit[3], F32R), at("A1_hi", BIG, unit[5], F32R)]
        A_lo = [at("A0_lo", BIG, unit[4], F32R), at("A1_lo", BIG, unit[6], F32R)]
        ZC = at("ZC", BIG, unit[3])
        B_hi = at("B_hi", BIG, unit[4], F32R)
        B_lo = at("B_lo", BIG, unit[5], F32R)
        RAW = at("RAW", 4 * TILE)
        W_hi = at("W_hi", 4 * HALF, dt=F32R)
        W_lo = at("W_lo", 4 * HALF, dt=F32R)
        KD = at("KD", NKV * S)
        V = at("V", NB * 2 * P)
        AW = at("AW", 4 * ADA_W)
        ACC = at("ACC", ADA_W)
        CS = at("CS", CST_COLS)
        PR = at("PR", PRM_COLS)
        MOD = at("MOD", 2 * 48)
        COL = at("COL", 96)
        SM = at("SM", 64)
        roped = cursor[0]
        ROPE = at("ROPE", 2 * S)
        PT1 = at("PT1", 2 * S, roped)
        sb1 = cursor[0]
        SB1 = at("SB1", 2 * 4 * 2 * P)
        KI = at("KI", S, sb1)
        WIS = at("WIS", S, sb1 + S * 4)
        WI = at("WI", NB * 8, sb1 + S * 8)
        XC = at("XC", S, sb1 + S * 12)
        SQ = at("SQ", 2 * S, unit[7] + S * 24)
        QR = at("QR", 3 * S, unit[4])
        QN = at("QN", 3 * S, unit[4] + S * 12)
        RAB = at("RAB", 2 * S, unit[6])
        SS = at("SS", S, unit[7] + S * 20)
        VC = at("VC", 2 * 24)
        G1 = at("G1", 2 * S)
        Y2 = at("Y2", 2 * S)
        qr1 = sb1
        QR1 = at("QR1", 2 * S, qr1)
        RAB1 = at("RAB1", 2 * S, qr1 + S * 8)
        YT = at("YT", 2 * P)
        LQ = G1
        assert cursor[0] <= nc.sbuf_usable_end, (cursor[0], nc.sbuf_usable_end)

        ps = [ctx.enter_context(nc.psum_tensor(f"bank{b}", [P, S], F32)) for b in range(8)]

        def sem(name):
            return ctx.enter_context(nc.semaphore(name))

        consts_in, x_in, lru_in, pos_in = sem("consts_in"), sem("x_in"), sem("lru_in"), sem("pos_in")
        rope_in = sem("rope_in")
        raw_in = [sem(f"raw_in{k}") for k in range(4)]
        ada_in = [sem(f"ada_in{k}") for k in range(4)]
        out_done = sem("out_done")
        hi_done, lo_done, used = sem("hi_done"), sem("lo_done"), sem("used")
        bank_free = [sem("bank_free0"), sem("bank_free1")]
        ada_used, ada_mm = sem("ada_used"), sem("ada_mm")
        dve_chain, act_chain, pool_chain = sem("dve_chain"), sem("act_chain"), sem("pool_chain")
        prm_done = sem("prm_done")
        x_new, sq_done, ss_step = sem("x_new"), sem("sq_done"), sem("ss_step")
        var_done, root_done, rinv_done = sem("var_done"), sem("root_done"), sem("rinv_done")
        stat_mm, t1_done, h_hi_done, h_lo_done = sem("stat_mm"), sem("t1_done"), sem("h_hi_done"), sem("h_lo_done")
        x_final = sem("x_final")
        u_done, gate_mm, gate_out = sem("u_done"), sem("gate_mm"), sem("gate_out")
        b2_done, root_b = sem("b2_done"), sem("root_b")
        ta_done, iu_done, states_done = sem("ta_done"), sem("iu_done"), sem("states_done")
        qraw, rot_mm, rope_done, v_done = sem("qraw"), sem("rot_mm"), sem("rope_done"), sem("v_done")
        ms_mm, qn_done = sem("ms_mm"), sem("qn_done")
        ki_step, wi_mm, wi_done = sem("ki_step"), sem("wi_mm"), sem("wi_done")
        xc_done, xsq_done = sem("xc_done"), sem("xsq_done")
        idx_mm, relu_done, relu_used = sem("idx_mm"), sem("relu_done"), sem("relu_used")
        fn_done, prod_done, a_hi_done, a_lo_done = sem("fn_done"), sem("prod_done"), sem("a_hi_done"), sem("a_lo_done")
        ga_done = sem("ga_done")
        qk_mm, ttr_done, negm_done = sem("qk_mm"), sem("ttr_done"), sem("negm_done")
        exp_done, norm_done = sem("exp_done"), sem("norm_done")
        pt_mm, pt_out, pv_mm, yt_out = sem("pt_mm"), sem("pt_out"), sem("pv_mm"), sem("yt_out")
        yy_done, y_hi_done, y_lo_done = sem("yy_done"), sem("y_hi_done"), sem("y_lo_done")

        def cs(name):
            a, n = CST[name]
            return CS[:, a:a + n]

        def pr(name, j=0, n=1):
            a, _ = PRM[name]
            return PR[:, ds(j + a, n)]

        def ch(t, j, n=S):
            return t[:, ds(j * S, n)]

        SPN = COL[:, 0:8]
        CACT = COL[:, 8:16]
        ONE = COL[:, 16:17]

        def gcol(layer, which, j):
            return COL[:, ds(j + (24 + 16 * layer + 8 * which), 1)]

        def mod(layer, m, j):
            return MOD[:, ds(j + (48 * layer + 8 * m), 1)]

        STEPS = att_steps(1) + att_steps(2)
        PT_COUNT = [0]
        for _, _, ks in STEPS:
            PT_COUNT.append(PT_COUNT[-1] + len(ks))

        block = ctx.enter_context(nc.Block())

        @block.sync
        def _(sp):
            def raw(tile, waits=True):
                if waits:
                    sp.wait_ge(lo_done, (tile.n - 3) * 2)
                sp.dma_start(RAW[:, tile.slot * TILE:(tile.slot + 1) * TILE],
                             stream[ds(tile.n, 1), :, :].rearrange("a p c -> (a p) c")).then_inc(raw_in[tile.slot], 16)

            def ada_load(a_static, a, waits=True):
                if waits:
                    sp.wait_ge(ada_used, a - 3)
                slot = a_static % 4
                sp.dma_start(AW[:, slot * ADA_W:(slot + 1) * ADA_W],
                             ada[ds(a, 1), :, :].rearrange("a p c -> (a p) c")).then_inc(ada_in[slot], 16)

            sp.dma_start(X[:], x).then_inc(x_in, 16)
            sp.dma_start(PR[:], prm).then_inc(consts_in, 16)
            sp.dma_start(CS[:], cst).then_inc(consts_in, 16)
            for n in range(4):
                raw(Tile(n), False)
            sp.dma_start(LW[:], lru_w).then_inc(lru_in, 16)
            sp.dma_start(ROPE[:], rope1).then_inc(rope_in, 16)
            for a in range(4):
                ada_load(a, a, False)
            a = 4
            last_ada = ADA_RANGES * KC

            def step(t0, i=0, t_next=None):
                raw(Tile(t0 + 4, i))

            with sp.Fori(0, 12) as i:
                q = 4
                for s in range(4):
                    raw(Tile(s + 4, i))
                    for _ in range(ADA_COUNT[s]):
                        if True:
                            ada_load(q, i * 8 + q)
                            q += 1
            for t in range(48, T_FFN0):
                raw(Tile(t + 4))
                if t == T_MA:
                    sp.wait_ge(pt_mm, PT_COUNT[16])
                    sp.wait_ge(pt_out, PT_COUNT[16])
                    sp.dma_start(SB1[:, 0:S].bitcast(I32), pos).then_inc(pos_in, 16)
            a0 = 100
            for kind, t0, bodies, with_ada in ffn_parts(T_FFN0, 0):
                with sp.Fori(0, bodies) as i:
                    q = 0
                    for s in range(4):
                        raw(Tile(t0 + s + 4, i))
                        if with_ada:
                            for _ in range(ADA_COUNT[s]):
                                ada_load(a0 + q, i * 8 + (a0 + q))
                                q += 1
                if with_ada:
                    a0 += 8 * bodies
            with sp.Fori(0, (T_END - 4 - T_CONV) // 4) as i:
                for s in range(4):
                    raw(Tile(T_CONV + s + 4, i))
            for j in range(KC):
                sp.wait_ge(x_final, j + 1)
                sp.dma_start(out[:, j * S:(j + 1) * S], ch(X, j)).then_inc(out_done, 16)
            sp.wait_ge(out_done, 16 * KC)

        @block.tensor
        def _(pe):
            def linear(tile, hi, lo, chunks=KC, first=None):
                dst = ps[tile.bank][:]
                if not (isinstance(tile.uses, int) and tile.uses == 0):
                    pe.wait_ge(bank_free[tile.bank], tile.uses)
                for half in range(2):
                    sl = (2 * tile.slot + half) % 4
                    pe.wait_ge(lo_done, tile.n * 2 + (half + 1))
                    ks = range(4 * half, min(4 * half + 4, chunks))
                    for k in ks:
                        if first is not None:
                            pe.wait_ge(*first(k))
                        c = sl * HALF + (k % 4) * P
                        wh, wl = W_hi[:, c:c + P], W_lo[:, c:c + P]
                        pe.matmul(dst, wh, ch(hi, k), start=(k == 0), stop=False)
                        pe.matmul(dst, wh, ch(lo, k), start=False, stop=False)
                        mm = pe.matmul(dst, wl, ch(hi, k), start=False, stop=(k == chunks - 1))
                    mm.then_inc(used, 1)

            def values(tile):
                pe.wait_ge(bank_free[tile.bank], tile.uses)
                for half in range(2):
                    pe.wait_ge(lo_done, tile.n * 2 + (half + 1))
                for n in range(NB):
                    dst = ps[tile.bank][:, n * P:(n + 1) * P]
                    for k in range(KC):
                        c = ((2 * tile.slot + k // 4) % 4) * HALF + (k % 4) * P
                        hh, hl = (t[:, k * S + n * P:k * S + (n + 1) * P] for t in (H_hi, H_lo))
                        pe.matmul(dst, hh, W_hi[:, c:c + P], start=(k == 0), stop=False)
                        pe.matmul(dst, hh, W_lo[:, c:c + P], start=False, stop=False)
                        mm = pe.matmul(dst, hl, W_hi[:, c:c + P], start=False, stop=(k == KC - 1))
                mm.then_inc(used, 2) if n == NB - 1 else None

            def ada_columns(r):
                pe.wait_ge(ada_used, ada_base[0] + 8 * 1 + r * 8)
                for q in range(4):
                    mm = pe.matmul(ps[7][:, ds(r * 4 + q, 1)], ACC[:, q * P:(q + 1) * P], ONE,
                                   start=True, stop=True)
                mm.then_inc(ada_mm, 1)

            ada_base = [0]

            def stat_columns(z, squares, sel, w):
                for n in range(NB):
                    mm = pe.matmul(ps[4][:, n * w:(n + 1) * w], squares[:, n * P:(n + 1) * P], sel,
                                   start=True, stop=True)
                mm.then_inc(stat_mm, 1)

            def stat_rows(z, w):
                pe.wait_ge(rinv_done, z + 1)
                for n in range(NB):
                    for k in range(w):
                        c, m = (z % 2) * 24 + 16 + n * w + k, P // w
                        mm = pe.matmul(ps[2][k * m:(k + 1) * m, n * P:(n + 1) * P],
                                       VC[:, c:c + 1].to_broadcast([P, m]), cs("ident"), start=True, stop=True)
                mm.then_inc(stat_mm, 1)

            def norm_stat(idx, z):
                pe.wait_ge(ss_step, 8 * (idx + 1))
                stat_columns(z, SS, cs("sel_all"), 1)
                stat_rows(z, 1)

            def gates(j):
                pe.wait_ge(u_done, j + 1)
                if j:
                    pe.wait_ge(gate_out, 2 * j)
                else:
                    pe.wait_ge(lru_in, 16)
                pe.matmul(ps[3][:], LW[:, j * P:(j + 1) * P], ch(U, j), start=True, stop=True)
                pe.matmul(ps[4][:], LW[:, (KC + j) * P:(KC + j + 1) * P], ch(U, j),
                          start=True, stop=True).then_inc(gate_mm, 1)

            def rot1(c):
                pe.wait_ge(qraw, c + 1)
                if c >= 2:
                    pe.wait_ge(rope_done, c - 1)
                pe.matmul(ps[5 + c % 2][:], cs("rot1"), ch(QR1, c % 2), start=True, stop=True).then_inc(rot_mm, 1)

            def qk(s):
                g, n, keys = STEPS[s]
                w = len(keys) * P
                for h in range(4):
                    half, chunk = h % 2, 2 * g + h // 2
                    if s < 16:
                        dst = ps[2 + half][:, (h // 2) * 256:(h // 2) * 256 + w]
                        if s and h == 0:
                            pe.wait_ge(ttr_done, 4 * s)
                    else:
                        dst = ps[2 + half][:, 0:w]
                        pe.wait_ge(ttr_done, 4 * s + h - 1)
                    rows = slice(64 * half, 64 * half + 64)
                    mm = pe.matmul(dst, Q[rows, chunk * S + n * P:chunk * S + (n + 1) * P],
                                   KD[rows, g * S + keys[0] * P:g * S + (keys[-1] + 1) * P],
                                   start=True, stop=True)
                    mm.then_inc(qk_mm, 1)

            PTB = {1: [4, 5], 2: [4, 5, 0, 1]}

            def turn_probs(s):
                g, n, keys = STEPS[s]
                w = len(keys) * P
                SB, width = (SB1, 2 * P) if s < 16 else (SB2, S)
                banks = PTB[1 if s < 16 else 2]
                pe.wait_ge(norm_done, 4 * s + 4)
                if s:
                    pe.wait_ge(pt_out, PT_COUNT[s])
                for c in range(len(keys)):
                    for h in range(4):
                        src = (s % 2) * 4 * width + h * w + c * P
                        mm = pe.transpose(ps[banks[c]][:, h * P:(h + 1) * P], SB[:, src:src + P], cs("ident"))
                    mm.then_inc(pt_mm, 1)

            def pv(s):
                g, n, keys = STEPS[s]
                PT = PT1 if s < 16 else PT2
                if s:
                    pe.wait_ge(yt_out, s)
                for c, kb in enumerate(keys):
                    pe.wait_ge(pt_out, PT_COUNT[s] + c + 1)
                    mm = pe.matmul(ps[6][0:HD, :], V[:, kb * 2 * P + g * HD:kb * 2 * P + (g + 1) * HD],
                                   ch(PT, c), start=(c == 0), stop=(c == len(keys) - 1))
                mm.then_inc(pv_mm, 1)

            pe.wait_ge(consts_in, 32)
            norm_stat(0, 0)

            def h_ready(idx):
                return lambda k: (h_lo_done, 8 * idx + k + 1)

            for t in range(T_U, T_Q):
                linear(Tile(t), H_hi, H_lo, first=h_ready(0) if t == 0 else None)
                if t:
                    gates(t - 1)
                if t % 4 == 3:
                    ada_columns(t // 4)
            for c in range(10):
                t = T_Q + c
                linear(Tile(t), H_hi, H_lo)
                if c == 0:
                    gates(7)
                else:
                    if c == 1:
                        pe.wait_ge(rope_in, 16)
                    rot1(c - 1)
                if t % 4 == 3:
                    ada_columns(t // 4)
            for t in range(T_V, T_GA):
                values(Tile(t))
                if t == T_V:
                    rot1(9)
                if t % 4 == 3:
                    ada_columns(t // 4)
            linear(Tile(T_GA), H_hi, H_lo)
            pe.wait_ge(rope_done, 10)
            qk(0)
            linear(Tile(T_GA + 1), H_hi, H_lo)

            def filler(t, kind, j):
                if kind == "R":
                    linear(Tile(t), YR_hi, YR_lo, first=(lambda k: (a_lo_done, k + 1)) if j == 0 else None)
                else:
                    linear(Tile(t), H_hi, H_lo)
                if t % 4 == 3 and t < 48:
                    ada_columns(t // 4)

            for s in range(16):
                pair = FILL[s] if s < len(FILL) else []
                if pair:
                    filler(T_FILL + 2 * s, *pair[0])
                turn_probs(s)
                if s < 15:
                    qk(s + 1)
                if pair:
                    filler(T_FILL + 2 * s + 1, *pair[1])
                if s == 0:
                    pe.wait_ge(v_done, 2)
                pv(s)

            def ma_body(i):
                for q in range(4):
                    tile = Tile(T_MA + q, i)
                    if q % 2 == 0:
                        linear(tile, H_hi, H_lo)
                    else:
                        linear(tile, YA_hi, YA_lo,
                               first=(lambda k: (y_lo_done, 16)) if q == 1 and isinstance(i, int) else None)

            ma_body(0)
            with pe.Fori(1, 4) as i:
                ma_body(i)
            for q in range(8):
                linear(Tile(T_WO + q), MG_hi, MG_lo,
                       first=(lambda k: (a_lo_done, 16 - 8 + k + 1)) if q == 0 else None)
            norm_stat(1, 1)
            norm_stat(2, 2)

            def mean_square(c):
                pe.wait_ge(qraw, QRAW(c))
                pe.wait_ge(var_done, 3 + c)
                stat_columns(3 + c, ch(SQ, c % 2), cs("sel_head"), 2)

            def inverse_root(c):
                pe.wait_ge(qn_done, QN_N(c))
                stat_rows(3 + c, 2)

            def rot2(c):
                pe.wait_ge(qn_done, QN_N(c + 1))
                if c >= 1:
                    pe.wait_ge(rope_done, ROPES(c))
                pe.matmul(ps[3][:], cs("rot2"), ch(QN, c % 3), start=True, stop=True).then_inc(rot_mm, 1)

            for c in range(20):
                if c < 17:
                    t = T_QKV2 + c
                    if ITEMS2[c] == "v":
                        values(Tile(t))
                    else:
                        linear(Tile(t), H_hi, H_lo, first=h_ready(1) if c == 0 else None)
                if 1 <= c < 17 and ITEMS2[c - 1] in ("q", "k"):
                    mean_square(c - 1)
                if 2 <= c < 17 and ITEMS2[c - 2] in ("q", "k"):
                    inverse_root(c - 2)
                if 3 <= c < 19 and ITEMS2[c - 3] in ("q", "k", "qi"):
                    rot2(c - 3)
            pe.wait_ge(ki_step, 1)
            pe.matmul(ps[2][:], cs("mean_head"), ch(QR, 0), start=True, stop=True).then_inc(ms_mm, 1)
            pe.wait_ge(wi_done, 1)
            for n in range(NB):
                mm = pe.transpose(ps[5][:, n * 8:(n + 1) * 8], WIS[64:72, n * P:(n + 1) * P],
                                  CS[64:72, CST["ident"][0] + 64:CST["ident"][0] + 72])
            mm.then_inc(wi_mm, 1)
            pe.wait_ge(xsq_done, 3)
            stat_columns(13, ch(SQ, 0), cs("sel_head"), 2)
            stat_rows(13, 2)
            pe.wait_ge(qn_done, QN_N(17))
            pe.matmul(ps[3][:], cs("rot2"), ch(QN, 0), start=True, stop=True).then_inc(rot_mm, 1)
            pe.wait_ge(rope_done, ROPES(17))
            m = 0
            for n in range(1, NB):
                for h in range(8):
                    rows = slice(64 * (h % 2), 64 * (h % 2) + 64)
                    if m >= 2:
                        pe.wait_ge(relu_done, m - 1)
                    elif m == 0:
                        pe.wait_ge(wi_done, 2)
                    pe.matmul(ps[4 + m % 2][:, 0:(n + 1) * P],
                              QI[rows, (h // 2) * S + n * P:(h // 2) * S + (n + 1) * P],
                              KI[rows, 0:(n + 1) * P], start=True, stop=True).then_inc(idx_mm, 1)
                    m += 1
            pe.wait_ge(relu_done, 24)
            pe.wait_ge(bank_free[0], Tile(T_AO2 + T_AO2 % 2).uses)
            pe.wait_ge(bank_free[1], Tile(T_AO2 + 1 - T_AO2 % 2).uses)
            pe.wait_ge(v_done, 4)
            qk(16)
            for s in range(16, 32):
                turn_probs(s)
                if s < 31:
                    qk(s + 1)
                pv(s)
            pe.wait_ge(pt_out, PT_COUNT[32])
            for q in range(8):
                linear(Tile(T_AO2 + q), YA_hi, YA2_lo, first=(lambda k: (y_lo_done, 32)) if q == 0 else None)
            norm_stat(3, 14)

            def segment(t0, bodies, hi, lo, chunks=KC, first=None, with_ada=False, r0=0):
                def body(i, f):
                    for q in range(4):
                        linear(Tile(t0 + q, i), hi, lo, chunks, first=f if q == 0 else None)
                    if with_ada:
                        ada_columns(i + r0)
                body(0, first)
                if bodies > 1:
                    with pe.Fori(1, bodies) as i:
                        body(i, None)

            def ffn(t_first, layer, idx, pairs0):
                r0 = 0
                for kind, t0, bodies, with_ada in ffn_parts(t_first, layer):
                    if kind[0] == "gu":
                        segment(t0, bodies, H_hi, H_lo, first=h_ready(idx) if kind[1] == 0 else None,
                                with_ada=with_ada, r0=r0)
                    else:
                        g = kind[1]
                        need = pairs0 + sum(FFN_GROUPS[:g])
                        segment(t0, bodies, A_hi[g % 2], A_lo[g % 2], FFN_GROUPS[g],
                                first=lambda k, need=need: (a_lo_done, need + k + 1), with_ada=with_ada, r0=r0)
                    if with_ada:
                        r0 += bodies

            ada_base[0] = ADA_RANGES * KC
            ffn(T_FFN0, 0, 2, 16)
            norm_stat(4, 15)
            segment(T_CONV, 4, H_hi, H_lo, first=h_ready(3))
            segment(T_CONVB, 2, H_hi, H_lo)
            segment(T_CO, 2, B_hi, B_lo, first=lambda k: (a_lo_done, 16 + 22 + k + 1))
            norm_stat(5, 16)
            ffn(T_FFN1, 1, 4, 16 + 22 + 8)

        @block.scalar
        def _(act):
            chain = Tally(act_chain)

            def split_hi(tile):
                act.wait_ge(raw_in[tile.slot], tile.turn * 16 + 16)
                for half in range(2):
                    sl = (2 * tile.slot + half) % 4
                    if not (isinstance(tile.n, int) and 2 * tile.n + half < 4):
                        act.wait_ge(used, tile.n * 2 + (half - 3))
                    c = tile.slot * TILE + half * HALF
                    act.copy(W_hi[:, sl * HALF:(sl + 1) * HALF], RAW[:, c:c + HALF]).then_inc(hi_done, 1)

            def ready(tile):
                act.wait_ge(used, tile.n * 2 + 2)

            def square(k, c, source=X):
                if not (isinstance(c, int) and c < 2):
                    act.wait_ge(ss_step, c - 1)
                act.activation(ch(SQ, k % 2 if isinstance(k, int) else 0), ch(source, k), ACT.Square).then_inc(sq_done, 1)

            def root(z, w):
                act.wait_ge(var_done, z + 1)
                a = (z % 2) * 24
                act.activation(VC[:, a + 8:a + 8 + 4 * w], VC[:, a:a + 4 * w], ACT.Sqrt).then_inc(root_done, 1)

            def norm_hi(idx, shift=None):
                for k in range(KC):
                    act.wait_ge(t1_done, 8 * idx + k + 1)
                    if shift is None:
                        ins = act.copy(ch(H_hi, k), ch(G1, k % 2))
                    else:
                        ins = act.activation(ch(H_hi, k), ch(G1, k % 2), ACT.Identity, bias=shift(k))
                    ins.then_inc(h_hi_done, 1)

            def gate_fn(tile, fn, p, dst=None):
                ready(tile)
                if not (isinstance(p, int) and p < 2):
                    act.wait_ge(prod_done, p - 1)
                par = p % 2 if isinstance(p, int) else dst
                act.activation(ch(G1, par), ps[tile.bank][:], fn).then_inc(fn_done, 1)

            def product_hi(dst, p, par):
                act.wait_ge(prod_done, p + 1)
                act.copy(dst, ch(Y2, par)).then_inc(a_hi_done, 1)

            act.wait_ge(consts_in, 32)
            act.activation(CACT, pr("c", 0, 8), ACT.Silu).then_inc(prm_done, 1)
            act.wait_ge(prm_done, 2)
            act.activation(COL[:, 88:96], COL[:, 80:88], ACT.Exp).then_inc(prm_done, 1)
            act.wait_ge(x_in, 16)
            for k in range(KC):
                square(k, k)
            root(0, 1)
            split_hi(Tile(0))
            norm_hi(0)
            for t in range(T_U, T_Q):
                split_hi(Tile(t + 1))
                if t:
                    j = t - 1
                    act.wait_ge(gate_mm, j + 1)
                    act.activation(ch(R, j), ps[3][:], ACT.Sigmoid, bias=pr("b_a", j)).then_inc(gate_out, 1)
                    act.activation(ch(I, j), ps[4][:], ACT.Sigmoid, bias=pr("b_x", j)).then_inc(gate_out, 1)

            def evac1(c):
                tile = Tile(T_Q + c)
                ready(tile)
                if c >= 2:
                    act.wait_ge(rope_done, c - 1)
                act.copy(ch(QR1, c % 2), ps[tile.bank][:]).then_inc(qraw, 1)
                act.wait_ge(qraw, c + 1)
                act.sem_inc(bank_free[tile.bank], 1)

            def roots_b(j0, j1):
                for j in range(j0, j1):
                    act.wait_ge(b2_done, j + 1)
                    act.activation(ch(T, j), ch(T, j), ACT.Sqrt).then_inc(root_b, 1)

            def tanh_exp(j):
                act.wait_ge(prm_done, 5)
                act.activation(ch(T, j), ch(R, j), ACT.Tanh, scale=SPN[:, j:j + 1]).then_inc(ta_done, 1)
                act.wait_ge(ta_done, 2 * j + 1)
                act.activation(ch(R, j), ch(R, j), ACT.Exp, scale=COL[:, 72 + j:73 + j]).then_inc(ta_done, 1)

            for c in range(10):
                split_hi(Tile(T_Q + c + 1))
                if c == 0:
                    act.wait_ge(gate_mm, 8)
                    act.activation(ch(R, 7), ps[3][:], ACT.Sigmoid, bias=pr("b_a", 7)).then_inc(gate_out, 1)
                    act.activation(ch(I, 7), ps[4][:], ACT.Sigmoid, bias=pr("b_x", 7)).then_inc(gate_out, 1)
                    act.wait_ge(gate_out, 16)
                if c < 8:
                    tanh_exp(c)
                evac1(c)
                if c == 9:
                    roots_b(0, 2)

            def values_out(tile, v, col):
                ready(tile)
                act.copy(V[:, :].rearrange("p (n c) -> p n c", c=2 * P)[:, :, col * P:(col + 1) * P],
                         ps[tile.bank][:].rearrange("p (n c) -> p n c", c=P)).then_inc(v_done, 1)
                act.wait_ge(v_done, v + 1)
                act.sem_inc(bank_free[tile.bank], 1)

            for v in range(2):
                split_hi(Tile(T_V + v + 1))
                values_out(Tile(T_V + v), v, v)
                roots_b(2 + 3 * v, 5 + 3 * v)

            def exps(s):
                g, n, keys = STEPS[s]
                w = len(keys) * P
                SB, width = (SB1, 2 * P) if s < 16 else (SB2, S)
                m = (s % 2) * 24
                act.wait_ge(negm_done, s + 1)
                for h in range(4):
                    a = (s % 2) * 4 * width + h * w
                    act.activation(SB[:, a:a + w], SB[:, a:a + w], ACT.Exp, bias=SM[:, m + 4 + h:m + 5 + h],
                                   accum_out=SM[:, m + 8 + h:m + 9 + h]).then_inc(exp_done, 1)
                if s < 16:
                    act.activation(SM[:, m + 12:m + 16], SM[:, m + 12:m + 16], ACT.Exp).then_inc(exp_done, 1)

            def probs_out(s):
                g, n, keys = STEPS[s]
                PT = PT1 if s < 16 else PT2
                banks = [4, 5, 0, 1]
                if s:
                    act.wait_ge(pv_mm, s)
                for c in range(len(keys)):
                    act.wait_ge(pt_mm, PT_COUNT[s] + c + 1)
                    act.copy(ch(PT, c), ps[banks[c]][:]).then_inc(pt_out, 1)

            def heads_out(s):
                act.wait_ge(pv_mm, s + 1)
                if s:
                    act.wait_ge(y_lo_done, s)
                src = ps[6][0:HD, :].rearrange("p (a b t) -> p a b t", a=2, b=2)
                dst = YT[:, :].rearrange("p (a t) -> p a t", a=2)
                act.copy(dst[0:HD], src[:, :, 0, :]).then_inc(act_chain, 1)
                chain.n += 1
                act.copy(dst[HD:P], src[:, :, 1, :]).then_inc(yt_out, 1)

            def y_region(t, s):
                g, n, _ = STEPS[s]
                return t[:, :].rearrange("p (k t) -> p k t", t=S)[:, 2 * g:2 * g + 2, n * P:(n + 1) * P]

            def heads_hi(s):
                if s < 16:
                    act.wait_ge(yy_done, s + 1)
                else:
                    act.wait_ge(yt_out, s + 1)
                    act.wait_ge(act_chain, chain.n)
                act.copy(y_region(YA_hi, s), YT[:, :].rearrange("p (k t) -> p k t", k=2)).then_inc(y_hi_done, 1)

            fn_count = [0]

            def ga_out(t, j):
                ready(Tile(t))
                if j == 0:
                    act.wait_ge(states_done, 8)
                act.activation(ch(GA, j), ps[t % 2][:], ACT.Silu).then_inc(ga_done, 1)
                ga_n[0] += 1
                act.wait_ge(ga_done, ga_n[0])
                act.sem_inc(bank_free[t % 2], 1)

            ga_n = [0]
            for q in range(2):
                split_hi(Tile(T_GA + q + 1))
                ga_out(T_GA + q, q)

            p = [0]
            y = [0]

            def fn_free(t):
                fn_count[0] += 1
                act.wait_ge(fn_done, fn_count[0])
                act.sem_inc(bank_free[t % 2], 1)

            def fill_out(t, kind, j):
                if kind == "ga":
                    ga_out(t, j)
                elif kind == "gr":
                    gate_fn(Tile(t), ACT.Silu, p[0])
                    fn_free(t)
                    product_hi(ch(YR_hi, j), p[0], p[0] % 2)
                    p[0] += 1
                elif kind == "mr":
                    gate_fn(Tile(t), ACT.Sigmoid, p[0])
                    fn_free(t)
                else:
                    p[0] += 1

            for s in range(16):
                pair = FILL[s] if s < len(FILL) else []
                exps(s)
                if pair:
                    split_hi(Tile(T_FILL + 2 * s + 1))
                    fill_out(T_FILL + 2 * s, *pair[0])
                probs_out(s)
                if pair:
                    split_hi(Tile(T_FILL + 2 * s + 2))
                    fill_out(T_FILL + 2 * s + 1, *pair[1])
                heads_out(s)
                heads_hi(s)

            def pair_body(t0, i, fn, p0, dst_hi, b0, hi_of=None):
                for q in range(2):
                    ga, gb = Tile(t0 + 2 * q, i), Tile(t0 + 2 * q + 1, i)
                    pn = i * 2 + (p0 + q)
                    par = (p0 + q) % 2
                    split_hi(ga.next())
                    ready(ga)
                    act.wait_ge(prod_done, pn - 1)
                    act.activation(ch(G1, par), ps[ga.bank][:], fn).then_inc(fn_done, 1)
                    act.wait_ge(fn_done, i * 2 + (b0 + q + 1))
                    act.sem_inc(bank_free[ga.bank], 1)
                    split_hi(gb.next())
                    if dst_hi is not None:
                        product_hi(ch(dst_hi, i * 2 + q), pn, par)

            assert p[0] == 16 and fn_count[0] == 16
            act.wait_ge(xc_done, 1)
            act.activation(ROPE[:, 0:S], Y2[:, 0:S], ACT.Sin).then_inc(xsq_done, 1)
            act.activation(ROPE[:, S:2 * S], Y2[:, S:2 * S], ACT.Sin).then_inc(xsq_done, 1)
            with act.Fori(0, 4) as i:
                pair_body(T_MA, i, ACT.Sigmoid, 16, MG_hi, 16)
            for k in range(KC):
                split_hi(Tile(T_WO + k + 1))
                act.wait_ge(x_new, k + 1)
                square(k, 8 + k)
            root(1, 1)
            for k in range(KC):
                act.wait_ge(x_new, 8 + k + 1)
                square(k, 16 + k)
            root(2, 1)
            norm_hi(1, lambda k: mod(0, 0, k))
            nq = 0
            for c in range(17):
                tile = Tile(T_QKV2 + c)
                split_hi(tile.next())
                kind = ITEMS2[c]
                if kind == "v":
                    values_out(tile, 2 + c - 10, c - 10)
                    if c == 10:
                        root(3 + 9, 2)
                    continue
                ready(tile)
                if kind in ("q", "k"):
                    if c >= 3:
                        act.wait_ge(qn_done, QN_N(c - 2))
                    if c >= 2:
                        act.wait_ge(var_done, 3 + c - 1)
                    act.activation(ch(SQ, c % 2), ps[tile.bank][:], ACT.Square).then_inc(act_chain, 1)
                    chain.n += 1
                    ins = act.copy(ch(QR, c % 3), ps[tile.bank][:])
                    ins.then_inc(qraw, 1)
                elif kind == "qi":
                    act.wait_ge(rope_done, ROPES(c - 2))
                    act.wait_ge(qn_done, QN_N(c))
                    ins = act.copy(ch(QN, c % 3), ps[tile.bank][:])
                    ins.then_inc(qraw, 1)
                else:
                    act.wait_ge(qn_done, QN_N(12))
                    act.copy(ch(QR, 0), ps[tile.bank][:]).then_inc(ki_step, 1)
                    act.mul(WIS[64:72, :], ps[tile.bank][64:72, :], 8 ** -0.5 * HD ** -0.5).then_inc(wi_done, 1)
                    act.wait_ge(ki_step, 1)
                    act.wait_ge(wi_done, 1)
                    act.sem_inc(bank_free[tile.bank], 1)
                    continue
                nq += 1
                act.wait_ge(qraw, 10 + nq)
                act.wait_ge(act_chain, chain.n)
                act.sem_inc(bank_free[tile.bank], 1)
                if kind == "qi":
                    act.sem_inc(qn_done, 1)
                elif c:
                    root(3 + c - 1, 2)
            act.wait_ge(xc_done, 2)
            act.activation(ch(SQ, 0), XC[:, :], ACT.Square).then_inc(act_chain, 1)
            chain.n += 1
            act.wait_ge(act_chain, chain.n)
            act.sem_inc(xsq_done, 1)
            root(13, 2)
            act.wait_ge(wi_mm, 1)
            act.copy(WI[:, :], ps[5][:, 0:32]).then_inc(wi_done, 1)
            for m, (n, h) in enumerate((n, h) for n in range(1, NB) for h in range(8)):
                act.wait_ge(idx_mm, m + 1)
                if m >= 2:
                    act.wait_ge(relu_used, m - 1)
                act.activation(RL[:, (m % 2) * S:(m % 2) * S + (n + 1) * P], ps[4 + m % 2][:, 0:(n + 1) * P],
                               ACT.Relu).then_inc(relu_done, 1)
            for s in range(16, 32):
                exps(s)
                probs_out(s)
                heads_out(s)
                heads_hi(s)

            def residual_squares(t0, c0, shift):
                for k in range(KC):
                    split_hi(Tile(t0 + k + 1))
                    act.wait_ge(x_new, c0 - 8 + k + 1)
                    square(k, c0 + k)

            residual_squares(T_AO2, 24, None)
            root(14, 1)
            norm_hi(2, lambda k: mod(0, 3, k))

            def ffn(t_first, layer, pairs0, c0):
                pn = pairs0
                for kind, t0, bodies, _ in ffn_parts(t_first, layer):
                    if kind[0] == "gu":
                        with act.Fori(0, bodies) as i:
                            pair_body(t0, i, ACT.Silu, pn, A_hi[kind[1] % 2], pn)
                        pn += 2 * bodies
                    elif kind[1] < 2:
                        with act.Fori(0, bodies) as i:
                            for q in range(4):
                                split_hi(Tile(t0 + q + 1, i))
                    elif layer == 0:
                        residual_squares(t0, c0, None)
                    else:
                        for q in range(7):
                            split_hi(Tile(t0 + q + 1))

            ffn(T_FFN0, 0, 24, 32)
            root(15, 1)
            norm_hi(3, lambda k: mod(1, 0, k))
            with act.Fori(0, 4) as i:
                pair_body(T_CONV, i, ACT.Copy, 24 + 22, None, 24 + 22)
            with act.Fori(0, 2) as i:
                for q in range(4):
                    split_hi(Tile(T_CONVB + q + 1, i))
                    product_hi(ch(B_hi, i * 4 + q), i * 4 + (24 + 22 + 8 + q), q % 2)
            residual_squares(T_CO, 40, None)
            root(16, 1)
            norm_hi(4, lambda k: mod(1, 3, k))
            ffn2_p = 24 + 22 + 8 + 8
            pn = ffn2_p
            fnn = 24 + 22 + 8
            for kind, t0, bodies, _ in ffn_parts(T_FFN1, 1):
                if kind[0] == "gu":
                    with act.Fori(0, bodies) as i:
                        pair_body(t0, i, ACT.Silu, pn, A_hi[kind[1] % 2], fnn)
                    pn += 2 * bodies
                    fnn += 2 * bodies
                elif kind[1] < 2:
                    with act.Fori(0, bodies) as i:
                        for q in range(4):
                            split_hi(Tile(t0 + q + 1, i))
                else:
                    for q in range(7):
                        split_hi(Tile(t0 + q + 1))

        @block.gpsimd
        def _(pool):
            for j in range(KC):
                pool.wait_ge(gate_out, 2 * KC)
                pool.wait_ge(u_done, j + 1)
                pool.tensor_tensor(ch(I, j), ch(I, j), ch(U, j), ALU.mult).then_inc(iu_done, 1)

        @block.vector
        def _(dve):
            chain = Tally(dve_chain)

            def link(ins):
                chain.up(ins)
                dve.wait_ge(dve_chain, chain.n)

            def split_lo(tile):
                for half in range(2):
                    sl = (2 * tile.slot + half) % 4
                    dve.wait_ge(hi_done, tile.n * 2 + (half + 1))
                    c = tile.slot * TILE + half * HALF
                    w = slice(sl * HALF, (sl + 1) * HALF)
                    dve.tensor_tensor(W_lo[:, w], RAW[:, c:c + HALF], W_hi[:, w], ALU.subtract).then_inc(lo_done, 1)

            def ready(tile):
                dve.wait_ge(used, tile.n * 2 + 2)

            ada_state = [0, 0]

            def ada_tile(q, a, first_of_all=False, tally=None):
                dve.wait_ge(ada_in[q % 4], ada_turn(a, q))
                w = AW[:, (q % 4) * ADA_W:(q % 4 + 1) * ADA_W]
                if q == 0:
                    if not first_of_all:
                        dve.wait_ge(ada_mm, ada_state[1])
                    ins = dve.tensor_scalar(ACC[:, :], w, CACT[:, 0:1], None, ALU.mult)
                else:
                    dve.wait_ge(ada_used, a)
                    ins = dve.scalar_tensor_tensor(out=ACC[:, :], in0=w, scalar=CACT[:, q:q + 1], in1=ACC[:, :],
                                                   op0=ALU.mult, op1=ALU.add)
                ins.then_inc(ada_used, 1)

            def ada_turn(a, q):
                return ada_state[1] * 32 + (16 * (q // 4) + 16)

            def ada_step(t_in_body, r):
                ada_state[1] = r
                q0 = sum(ADA_COUNT[:t_in_body])
                for q in range(q0, q0 + ADA_COUNT[t_in_body]):
                    ada_tile(q, r * 8 + q, first_of_all=isinstance(r, int) and r == 0)

            def sum_square(c, first):
                dve.wait_ge(sq_done, c + 1)
                if first:
                    ins = dve.tensor_copy(SS[:, :], ch(SQ, c % 2))
                else:
                    dve.wait_ge(ss_step, c)
                    ins = dve.tensor_tensor(SS[:, :], SS[:, :], ch(SQ, c % 2), ALU.add)
                ins.then_inc(ss_step, 1)

            def variance(z, w):
                dve.wait_ge(stat_mm, STAT_COLS(z))
                a = (z % 2) * 24
                dve.tensor_scalar(VC[:, a:a + 4 * w], ps[4][:, 0:4 * w], EPS, None, ALU.add).then_inc(var_done, 1)

            def inverse(z, w):
                dve.wait_ge(root_done, z + 1)
                a = (z % 2) * 24
                v, r, t = VC[:, a:a + 4 * w], VC[:, a + 16:a + 16 + 4 * w], VC[:, a + 8:a + 8 + 4 * w]
                link(dve.reciprocal(r, t))
                link(dve.tensor_tensor(t, r, r, ALU.mult))
                link(dve.tensor_tensor(t, t, v, ALU.mult))
                link(dve.tensor_scalar(t, t, -0.5, 1.5, ALU.mult, ALU.add))
                dve.tensor_tensor(r, r, t, ALU.mult).then_inc(rinv_done, 1)

            def inv_rms(z):
                variance(z, 1)
                inverse(z, 1)
                dve.wait_ge(stat_mm, STAT_ROWS(z))

            def norm_lo(idx, gain, shift=None):
                def lo(k):
                    dve.wait_ge(h_hi_done, 8 * idx + k + 1)
                    if shift is None:
                        ins = dve.tensor_tensor(ch(H_lo, k), ch(G1, k % 2), ch(H_hi, k), ALU.subtract)
                    else:
                        ins = dve.scalar_tensor_tensor(out=ch(H_lo, k), in0=ch(G1, k % 2), scalar=shift(k),
                                                       in1=ch(H_hi, k), op0=ALU.add, op1=ALU.subtract)
                    ins.then_inc(h_lo_done, 1)
                for k in range(KC):
                    if k >= 2:
                        dve.wait_ge(h_lo_done, 8 * idx + k - 1)
                    dve.scalar_tensor_tensor(out=ch(G1, k % 2), in0=ch(X, k), scalar=gain(k), in1=ps[2][:],
                                             op0=ALU.mult, op1=ALU.mult).then_inc(t1_done, 1)
                    if k:
                        lo(k - 1)
                lo(KC - 1)

            dve.wait_ge(consts_in, 32)
            dve.memset(ONE, 1.0)
            lam = pr("lam", 0, 8)
            link(dve.tensor_scalar(COL[:, 72:80], lam, -1.0, None, ALU.mult))
            dve.tensor_tensor(COL[:, 80:88], COL[:, 72:80], lam, ALU.min).then_inc(prm_done, 1)
            dve.wait_ge(prm_done, 3)
            e = COL[:, 88:96]
            link(dve.tensor_scalar(COL[:, 80:88], e, 2.0, None, ALU.add))
            link(dve.reciprocal(COL[:, 80:88], COL[:, 80:88]))
            s_, s2, acc = COL[:, 88:96], COL[:, 80:88], COL[:, 0:8]
            link(dve.tensor_tensor(s_, e, s2, ALU.mult))
            link(dve.tensor_tensor(s2, s_, s_, ALU.mult))
            link(dve.memset(acc, 1.0 / 17))
            for odd in (15, 13, 11, 9, 7, 5, 3, 1):
                link(dve.tensor_tensor(acc, acc, s2, ALU.mult))
                link(dve.tensor_scalar(acc, acc, 1.0 / odd, None, ALU.add))
            link(dve.tensor_tensor(acc, acc, s_, ALU.mult))
            link(dve.tensor_scalar(COL[:, 72:80], COL[:, 72:80], 0.0, 8.0, ALU.max, ALU.mult))
            link(dve.scalar_tensor_tensor(out=acc, in0=acc, scalar=16.0, in1=COL[:, 72:80], op0=ALU.mult, op1=ALU.add))
            dve.tensor_scalar(COL[:, 72:80], acc, -1.0, None, ALU.mult).then_inc(prm_done, 2)

            for k in range(KC):
                sum_square(k, k == 0)
            inv_rms(0)
            split_lo(Tile(0))
            norm_lo(0, lambda k: pr("norm_g", k))

            for t in range(T_U, T_Q):
                split_lo(Tile(t + 1))
                tile = Tile(t)
                ready(tile)
                src = ps[tile.bank]
                link(dve.tensor_scalar(ch(U, t), src[:], pr("conv_w", 24 + t), pr("conv_b", t), ALU.mult, ALU.add))
                for d in (1, 2, 3):
                    dst = U[:, t * S + d:(t + 1) * S]
                    ins = dve.scalar_tensor_tensor(out=dst, in0=src[:, 0:S - d], scalar=pr("conv_w", 8 * (3 - d) + t),
                                                   in1=dst, op0=ALU.mult, op1=ALU.add)
                    if d < 3:
                        link(ins)
                ins.then_inc(u_done, 1)
                dve.wait_ge(u_done, t + 1)
                dve.sem_inc(bank_free[tile.bank], 1)
                ada_step(t % 4, t // 4)

            def lru_b(j):
                dve.wait_ge(ta_done, 2 * j + 2)
                link(dve.tensor_tensor(LQ[:, 0:S], ch(R, j), ch(R, j), ALU.mult))
                link(dve.scalar_tensor_tensor(out=ch(T, j), in0=LQ[:, 0:S], scalar=1.0, in1=ch(T, j),
                                              op0=ALU.add, op1=ALU.mult))
                dve.sem_inc(b2_done, 1)

            def lru_scan(j):
                dve.wait_ge(root_b, j + 1)
                dve.wait_ge(iu_done, j + 1)
                link(dve.tensor_tensor(ch(T, j), ch(T, j), ch(I, j), ALU.mult))
                dve.tensor_tensor_scan(ch(U, j), ch(R, j), ch(T, j), 0.0, ALU.mult, ALU.add).then_inc(states_done, 1)

            def rope1_out(c):
                dve.wait_ge(rot_mm, c + 1)
                if c == 0:
                    dve.wait_ge(rope_in, 16)
                dve.tensor_tensor(RAB1[:, 0:S], ch(QR1, c % 2), ROPE[:, 0:S], ALU.mult)
                link(dve.tensor_tensor(RAB1[:, S:2 * S], ps[5 + c % 2][:], ROPE[:, S:2 * S], ALU.mult))
                a, b = RAB1[:, 0:S], RAB1[:, S:2 * S]
                if c < 8:
                    link(dve.tensor_tensor(ch(Q, c), a, b, ALU.add))
                else:
                    add_keys(c - 8, a, b)
                dve.sem_inc(rope_done, 1)

            def add_keys(kc, a, b):
                for half in range(2):
                    rows = slice(64 * half, 64 * half + 64)
                    for other in range(2):
                        to = slice(64 * other, 64 * other + 64)
                        link(dve.tensor_tensor(KD[to, (2 * kc + half) * S:(2 * kc + half + 1) * S],
                                               a[rows, :], b[rows, :], ALU.add))

            for c in range(10):
                t = T_Q + c
                split_lo(Tile(t + 1))
                if c:
                    rope1_out(c - 1)
                    if c < 9:
                        lru_b(c - 1)
                ada_step(t % 4, t // 4)
            for t in range(T_V, T_GA):
                split_lo(Tile(t + 1))
                if t == T_V:
                    rope1_out(9)
                    lru_scan(0)
                    lru_scan(1)
                else:
                    for j in range(2, 5):
                        lru_scan(j)
                ada_step(t % 4, t // 4)

            def scores(s):
                g, n, keys = STEPS[s]
                w = len(keys) * P
                m = (s % 2) * 24
                if s >= 2:
                    dve.wait_ge(pt_mm, PT_COUNT[s - 1])
                for h in range(4):
                    if s < 16:
                        if h == 0:
                            dve.wait_ge(qk_mm, 4 * s + 4)
                        src = ps[2 + h % 2][:, (h // 2) * 256:(h // 2) * 256 + w]
                        mask = CS[:, CST["mask_diag"][0] - (w - P):CST["mask_diag"][0] + P]
                        start, SB, width = pr("sinks", 4 * g + h), SB1, 2 * P
                    else:
                        dve.wait_ge(qk_mm, 4 * s + h + 1)
                        src = ps[2 + h % 2][:, 0:w]
                        mask = BIAS[:, n * S:n * S + w]
                        start, SB, width = -3e38, SB2, S
                    a = (s % 2) * 4 * width + h * w
                    dve.tensor_tensor_reduce(out=SB[:, a:a + w], in0=src, in1=mask, scale=SCALE, scalar=start,
                                             op0=ALU.add, op1=ALU.max, accum_out=SM[:, m + h:m + h + 1]).then_inc(ttr_done, 1)
                dve.wait_ge(ttr_done, 4 * s + 4)
                if s < 16:
                    dve.tensor_tensor(SM[:, m + 12:m + 16], pr("sinks", 4 * g, 4), SM[:, m:m + 4],
                                      ALU.subtract).then_inc(dve_chain, 1)
                    chain.n += 1
                dve.tensor_scalar(SM[:, m + 4:m + 8], SM[:, m:m + 4], -1.0, None, ALU.mult).then_inc(dve_chain, 1)
                chain.n += 1
                dve.wait_ge(dve_chain, chain.n)
                dve.sem_inc(negm_done, 1)

            def normalise(s):
                g, n, keys = STEPS[s]
                w = len(keys) * P
                m = (s % 2) * 24
                SB, width = (SB1, 2 * P) if s < 16 else (SB2, S)
                dve.wait_ge(exp_done, 5 * min(s + 1, 16) + 4 * max(s + 1 - 16, 0))
                den = SM[:, m + 8:m + 12]
                if s < 16:
                    link(dve.tensor_tensor(den, den, SM[:, m + 12:m + 16], ALU.add))
                link(dve.reciprocal(SM[:, m + 16:m + 20], den))
                for h in range(4):
                    a = (s % 2) * 4 * width + h * w
                    dve.tensor_scalar(SB[:, a:a + w], SB[:, a:a + w], SM[:, m + 16 + h:m + 17 + h], None,
                                      ALU.mult).then_inc(norm_done, 1)

            def y_region(t, s):
                g, n, _ = STEPS[s]
                return t[:, :].rearrange("p (k t) -> p k t", t=S)[:, 2 * g:2 * g + 2, n * P:(n + 1) * P]

            def y_out(s):
                dve.wait_ge(yt_out, s + 1)
                yt = YT[:, :].rearrange("p (k t) -> p k t", k=2)
                if s < 16:
                    if s % 4 == 0:
                        dve.wait_ge(ga_done, GA_NEED[s // 4])
                    dve.tensor_tensor(yt, yt, y_region(GA, s), ALU.mult).then_inc(yy_done, 1)
                dve.wait_ge(y_hi_done, s + 1)
                dve.tensor_tensor(y_region(YA_lo if s < 16 else YA2_lo, s), yt, y_region(YA_hi, s), ALU.subtract).then_inc(y_lo_done, 1)

            GA_NEED = [2, 4, 6, 8]
            p, fnc = [0], [0]

            def fill_out(t, kind, j):
                par = p[0] % 2
                if kind != "ga" and y_n[0]:
                    dve.wait_ge(a_lo_done, y_n[0])
                if kind == "gr":
                    dve.wait_ge(fn_done, fnc[0] + 1)
                    fnc[0] += 1
                    dve.tensor_tensor(ch(Y2, par), ch(G1, par), ch(U, j), ALU.mult).then_inc(prod_done, 1)
                    dve.wait_ge(a_hi_done, y_n[0] + 1)
                    dve.tensor_tensor(ch(YR_lo, j), ch(Y2, par), ch(YR_hi, j), ALU.subtract).then_inc(a_lo_done, 1)
                    y_n[0] += 1
                    p[0] += 1
                elif kind == "R":
                    tile = Tile(t)
                    ready(tile)
                    dve.wait_ge(fn_done, fnc[0] + 1)
                    fnc[0] += 1
                    dve.tensor_tensor(ch(MG, j), ps[tile.bank][:], ch(G1, par), ALU.mult).then_inc(prod_done, 1)
                    p[0] += 1
                    dve.wait_ge(prod_done, p[0])
                    dve.sem_inc(bank_free[tile.bank], 1)

            y_n = [0]
            split_lo(Tile(T_GA + 1))
            for j in range(5, 8):
                lru_scan(j)
            dve.wait_ge(states_done, 8)
            ada_step(T_GA % 4, T_GA // 4)
            scores(0)
            split_lo(Tile(T_GA + 2))
            ada_step((T_GA + 1) % 4, (T_GA + 1) // 4)
            for s in range(16):
                pair = FILL[s] if s < len(FILL) else []
                normalise(s)
                for q in range(2):
                    t = T_FILL + 2 * s + q
                    if pair:
                        split_lo(Tile(t + 1))
                        fill_out(t, *pair[q])
                        if t < 48:
                            ada_step(t % 4, t // 4)
                    if q == 0 and s < 15:
                        scores(s + 1)
                y_out(s)

            def sin_tables():
                A, K = SB1[:, S:2 * S], SB1[:, 2 * S:3 * S]
                dve.wait_ge(pos_in, 16)
                dve.wait_ge(a_lo_done, 8)
                link(dve.tensor_copy(A, SB1[:, 0:S].bitcast(I32)))
                link(dve.tensor_scalar(A, A, cs("inv_freq"), None, ALU.mult))
                magic = 12582912.0
                link(dve.tensor_scalar(K, A, 1.0 / (2 * math.pi), magic, ALU.mult, ALU.add))
                link(dve.tensor_scalar(K, K, -magic, None, ALU.add))
                for part in TWO_PI_PARTS:
                    link(dve.scalar_tensor_tensor(out=A, in0=K, scalar=-part, in1=A, op0=ALU.mult, op1=ALU.add))
                lim = 3.1415925
                link(dve.tensor_scalar(K, A, math.pi / 2, None, ALU.add))
                link(dve.tensor_scalar(A, A, lim, -lim, ALU.min, ALU.max))
                link(dve.tensor_scalar(Y2[:, S:2 * S], A, cs("sin_sign"), None, ALU.mult))
                link(dve.tensor_scalar(A, K, math.pi, -2 * math.pi, ALU.is_gt, ALU.mult))
                link(dve.tensor_tensor(K, K, A, ALU.add))
                link(dve.tensor_scalar(Y2[:, 0:S], K, lim, -lim, ALU.min, ALU.max))
                dve.sem_inc(xc_done, 1)

            def ma_body(i):
                for q in range(4):
                    tile = Tile(T_MA + q, i)
                    split_lo(tile.next())
                    if q % 2:
                        par = (q // 2) % 2
                        jj = i * 2 + q // 2
                        ready(tile)
                        dve.wait_ge(fn_done, i * 2 + (16 + q // 2 + 1))
                        dve.wait_ge(a_lo_done, i * 2 + (8 + q // 2))
                        link(dve.tensor_tensor(ch(Y2, par), ps[tile.bank][:], ch(G1, par), ALU.mult))
                        dve.sem_inc(bank_free[tile.bank], 1)
                        dve.tensor_tensor(ch(Y2, par), ch(Y2, par), ch(MG, jj), ALU.add).then_inc(prod_done, 1)
                        dve.wait_ge(a_hi_done, i * 2 + (8 + q // 2 + 1))
                        dve.tensor_tensor(ch(MG_lo, jj), ch(Y2, par), ch(MG_hi, jj), ALU.subtract).then_inc(a_lo_done, 1)

            sin_tables()
            dve.wait_ge(xsq_done, 2)
            with looped(dve, 4, chain, 2) as i:
                ma_body(i)

            for k in range(KC):
                tile = Tile(T_WO + k)
                split_lo(tile.next())
                ready(tile)
                dve.tensor_tensor(ch(X, k), ps[tile.bank][:], ch(X, k), ALU.add).then_inc(x_new, 1)
                dve.wait_ge(x_new, k + 1)
                dve.sem_inc(bank_free[tile.bank], 1)
                sum_square(8 + k, k == 0)
            inv_rms(1)
            for k in range(KC):
                dve.scalar_tensor_tensor(out=ch(X, k), in0=ch(X, k), scalar=pr("final_g", k), in1=ps[2][:],
                                         op0=ALU.mult, op1=ALU.mult).then_inc(x_new, 1)
            for k in range(KC):
                if k == 0:
                    dve.wait_ge(x_new, 16)
                sum_square(16 + k, k == 0)
            def modulation(layer):
                dve.wait_ge(ada_mm, ADA_RANGES * (layer + 1))
                link(dve.tensor_tensor(MOD[:, 48 * layer:48 * layer + 48], ps[7][:, 0:48], pr("ada_b", 48 * layer, 48), ALU.add))
                for which, name, m in ((0, "norm1_g", 1), (1, "norm2_g", 4)):
                    a = 24 + 16 * layer + 8 * which
                    link(dve.scalar_tensor_tensor(out=COL[:, a:a + 8], in0=MOD[:, 48 * layer + 8 * m:48 * layer + 8 * m + 8],
                                                  scalar=1.0, in1=pr(name, 8 * layer, 8), op0=ALU.add, op1=ALU.mult))

            modulation(0)
            inv_rms(2)
            norm_lo(1, lambda k: gcol(0, 0, k), lambda k: mod(0, 0, k))
            dve.wait_ge(xsq_done, 2)

            ms = [0]

            def head_norm(c):
                dve.wait_ge(stat_mm, STAT_ROWS(3 + c))
                dve.scalar_tensor_tensor(out=ch(QN, c % 3), in0=ch(QR, c % 3),
                                         scalar=pr("q_g" if ITEMS2[c] == "q" else "k_g"), in1=ps[2][:],
                                         op0=ALU.mult, op1=ALU.mult).then_inc(qn_done, 1)

            def rope2_out(c, r):
                dve.wait_ge(rot_mm, 10 + r + 1)
                dve.wait_ge(qn_done, QN_N(c + 1))
                a, b = RAB[:, 0:S], RAB[:, S:2 * S]
                link(dve.tensor_tensor(a, ch(QN, c % 3), ROPE[:, 0:S], ALU.mult))
                link(dve.tensor_tensor(b, ps[3][:], ROPE[:, S:2 * S], ALU.mult))
                kind = ITEMS2[c] if c < 16 else "ki"
                if kind == "q":
                    link(dve.tensor_tensor(ch(Q, c), a, b, ALU.add))
                elif kind == "k":
                    add_keys(c - 8, a, b)
                elif kind == "qi":
                    link(dve.tensor_tensor(ch(QI, c - 12), a, b, ALU.add))
                else:
                    for half in range(2):
                        link(dve.tensor_tensor(KI[64 * half:64 * half + 64, :], a[0:64, :], b[0:64, :], ALU.add))
                dve.sem_inc(rope_done, 1)

            r = 0
            for c in range(19):
                if c < 17:
                    split_lo(Tile(T_QKV2 + c + 1))
                if 1 <= c < 17 and ITEMS2[c - 1] in ("q", "k"):
                    variance(3 + c - 1, 2)
                if 2 <= c < 17 and ITEMS2[c - 2] in ("q", "k"):
                    head_norm(c - 2)
                if 1 <= c < 17 and ITEMS2[c - 1] in ("q", "k"):
                    inverse(3 + c - 1, 2)
                if 3 <= c < 19 and ITEMS2[c - 3] in ("q", "k", "qi"):
                    rope2_out(c - 3, r)
                    r += 1
            dve.wait_ge(ms_mm, 1)
            link(dve.tensor_tensor(XC[:, :], ch(QR, 0), ps[2][:], ALU.subtract))
            dve.sem_inc(xc_done, 1)
            variance(13, 2)
            inverse(13, 2)
            dve.wait_ge(stat_mm, STAT_ROWS(13))
            link(dve.scalar_tensor_tensor(out=XC[:, :], in0=XC[:, :], scalar=pr("ki_g"), in1=ps[2][:],
                                          op0=ALU.mult, op1=ALU.mult))
            dve.tensor_scalar(ch(QN, 0), XC[:, :], pr("ki_b"), None, ALU.add).then_inc(qn_done, 1)
            rope2_out(18, r)

            m = 0
            dve.wait_ge(wi_done, 2)
            for n in range(1, NB):
                w = (n + 1) * P
                dst = SCALL[:, (n - 1) * S:(n - 1) * S + w]
                for h in range(8):
                    dve.wait_ge(relu_done, m + 1)
                    rl = RL[:, (m % 2) * S:(m % 2) * S + w]
                    wcol = WI[:, n * 8 + h:n * 8 + h + 1]
                    if h == 0:
                        ins = dve.tensor_scalar(dst, rl, wcol, None, ALU.mult)
                    else:
                        dve.wait_ge(relu_used, m)
                        ins = dve.scalar_tensor_tensor(out=dst, in0=rl, scalar=wcol, in1=dst,
                                                       op0=ALU.mult, op1=ALU.add)
                    ins.then_inc(relu_used, 1)
                    m += 1
                dve.wait_ge(relu_used, m)
                link(dve.tensor_tensor(dst[:, w - P:w], dst[:, w - P:w], cs("mask_diag"), ALU.add))
            link(dve.tensor_copy(BIAS[:, 0:P], cs("mask_diag")))
            M8 = SM[:, 48:56]

            def select(n, rounds):
                w = (n + 1) * P
                score, work = SCALL[:, (n - 1) * S:(n - 1) * S + w], WORK[:, 0:w]
                for q in rounds:
                    link(dve.max(M8, score if q == 0 else work))
                    link(dve.match_replace(work, M8, score if q == 0 else work, TAKEN))
                    if q == TOPK // 8 - 1:
                        b = BIAS[:, n * S:n * S + w]
                        link(dve.tensor_tensor(b, work, score, ALU.is_equal))
                        link(dve.tensor_scalar(b, b, NEG, None, ALU.mult))

            scores(16)
            for s in range(16, 32):
                g, n, _ = STEPS[s]
                normalise(s)
                if n < NB - 1:
                    select(n + 1, range(4 * g, 4 * g + 4))
                if s < 31:
                    scores(s + 1)
                y_out(s)

            def residual(t0, c0, layer, m, x0):
                for k in range(KC):
                    tile = Tile(t0 + k)
                    split_lo(tile.next())
                    ready(tile)
                    dve.scalar_tensor_tensor(out=ch(X, k), in0=ps[tile.bank][:], scalar=mod(layer, m, k),
                                             in1=ch(X, k), op0=ALU.mult, op1=ALU.add).then_inc(x_new, 1)
                    dve.wait_ge(x_new, c0 - 8 + k + 1)
                    dve.sem_inc(bank_free[tile.bank], 1)
                    sum_square(c0 + k, k == 0)

            residual(T_AO2, 24, 0, 2, 0)
            inv_rms(14)
            norm_lo(2, lambda k: gcol(0, 1, k), lambda k: mod(0, 3, k))

            def swiglu_body(t0, i, p0, f0, y0, g, with_ada, r):
                for q in range(4):
                    tile = Tile(t0 + q, i)
                    split_lo(tile.next())
                    if q % 2:
                        h = q // 2
                        par = (p0 + h) % 2
                        jj = i * 2 + h
                        ready(tile)
                        dve.wait_ge(fn_done, i * 2 + (f0 + h + 1))
                        dve.wait_ge(a_lo_done, i * 2 + (y0 + h))
                        dve.tensor_tensor(ch(Y2, par), ps[tile.bank][:], ch(G1, par), ALU.mult).then_inc(prod_done, 1)
                        dve.wait_ge(a_hi_done, i * 2 + (y0 + h + 1))
                        dve.sem_inc(bank_free[tile.bank], 1)
                        dve.tensor_tensor(ch(A_lo[g % 2], jj), ch(Y2, par), ch(A_hi[g % 2], jj),
                                          ALU.subtract).then_inc(a_lo_done, 1)
                    if with_ada:
                        ada_step(q, i + r)

            def ffn(t_first, layer, p0, f0, y0, c0):
                r = ADA_RANGES
                for kind, t0, bodies, with_ada in ffn_parts(t_first, layer):
                    if kind[0] == "gu":
                        with dve.Fori(0, bodies) as i:
                            swiglu_body(t0, i, p0, f0, y0, kind[1], with_ada, r)
                        p0 += 2 * bodies
                        f0 += 2 * bodies
                        y0 += 2 * bodies
                    elif kind[1] < 2:
                        with looped(dve, bodies, chain, 4) as i:
                            for q in range(4):
                                tile = Tile(t0 + q, i)
                                split_lo(tile.next())
                                ready(tile)
                                xk = ch(X, i * 4 + q)
                                link(dve.scalar_tensor_tensor(out=xk, in0=ps[tile.bank][:],
                                                              scalar=mod(layer, 5, i * 4 + q), in1=xk,
                                                              op0=ALU.mult, op1=ALU.add))
                                dve.sem_inc(bank_free[tile.bank], 1)
                                if with_ada:
                                    ada_step(q, i + r)
                    elif layer == 0:
                        residual(t0, c0, layer, 5, 0)
                    else:
                        for k in range(KC):
                            tile = Tile(t0 + k)
                            if k < 7:
                                split_lo(tile.next())
                            ready(tile)
                            dve.scalar_tensor_tensor(out=ch(X, k), in0=ps[tile.bank][:], scalar=mod(layer, 5, k),
                                                     in1=ch(X, k), op0=ALU.mult, op1=ALU.add).then_inc(x_final, 1)
                            if k < 6:
                                dve.wait_ge(x_final, k + 1)
                                dve.sem_inc(bank_free[tile.bank], 1)
                    if with_ada:
                        r += bodies

            ffn(T_FFN0, 0, 24, 24, 16, 32)
            modulation(1)
            inv_rms(15)
            norm_lo(3, lambda k: gcol(1, 0, k), lambda k: mod(1, 0, k))

            with looped(dve, 4, chain, 2 * 3) as i:
                for q in range(4):
                    tile = Tile(T_CONV + q, i)
                    split_lo(tile.next())
                    if q % 2:
                        h = q // 2
                        par = h % 2
                        ready(tile)
                        dve.wait_ge(fn_done, i * 2 + (46 + h + 1))
                        z = ch(Y2, par)
                        link(dve.tensor_tensor(z, ps[tile.bank][:], ch(G1, par), ALU.mult))
                        dve.sem_inc(bank_free[tile.bank], 1)
                        j = i * 2 + h
                        link(dve.tensor_scalar(ch(ZC, j), z, pr("conv3_w", j + 16), None, ALU.mult))
                        for d in (1, 2):
                            dst = ZC[:, ds(j * S + d, S - d)]
                            ins = dve.scalar_tensor_tensor(out=dst, in0=Y2[:, par * S:par * S + S - d],
                                                           scalar=pr("conv3_w", j + 8 * (2 - d)),
                                                           in1=dst, op0=ALU.mult, op1=ALU.add)
                            if d == 1:
                                link(ins)
                        ins.then_inc(prod_done, 1)
                        dve.wait_ge(prod_done, i * 2 + (46 + h + 1))
            with dve.Fori(0, 2) as i:
                for q in range(4):
                    tile = Tile(T_CONVB + q, i)
                    split_lo(tile.next())
                    ready(tile)
                    par = q % 2
                    j = i * 4 + q
                    dve.wait_ge(a_lo_done, i * 4 + (16 + 22 + q))
                    dve.tensor_tensor(ch(Y2, par), ps[tile.bank][:], ch(ZC, j), ALU.mult).then_inc(prod_done, 1)
                    dve.wait_ge(a_hi_done, i * 4 + (16 + 22 + q + 1))
                    dve.sem_inc(bank_free[tile.bank], 1)
                    dve.tensor_tensor(ch(B_lo, j), ch(Y2, par), ch(B_hi, j), ALU.subtract).then_inc(a_lo_done, 1)
            residual(T_CO, 40, 1, 2, 0)
            inv_rms(16)
            norm_lo(4, lambda k: gcol(1, 1, k), lambda k: mod(1, 3, k))
            ffn(T_FFN1, 1, 62, 54, 46, 0)


TWO_PI_PARTS = []
_rest = 2 * math.pi
for _bits in (6, 12):
    _unit = 2.0 ** -_bits if not TWO_PI_PARTS else 2.0 ** -17
    _part = math.floor(_rest / _unit) * _unit
    TWO_PI_PARTS.append(_part)
    _rest -= _part
TWO_PI_PARTS.append(_rest)

ITEMS2 = ["q"] * 8 + ["k"] * 2 + ["v"] * 2 + ["qi"] * 4 + ["ki"]


def QN_N(c):
    return sum(1 for x in ITEMS2[:c] if x != "v")


def QRAW(c):
    return 10 + sum(1 for x in ITEMS2[:c + 1] if x in ("q", "k", "qi"))


def ROPES(c):
    return 10 + sum(1 for x in ITEMS2[:c] if x != "v")


def STAT_COLS(z):
    return {3: 7}.get(z, 2 * z if 3 < z <= 12 else 2 * z + 1)


def STAT_ROWS(z):
    return 2 * z + 3 if 3 <= z < 12 else 2 * z + 2


def ffn_parts(t0, layer):
    out = []
    for kind, tiles in ((("gu", 0), 16), (("gu", 1), 16), (("down", 0), 8), (("gu", 2), 12), (("down", 1), 8),
                        (("down", 2), 8)):
        out.append((kind, t0, tiles // 4, layer == 0 and kind in (("gu", 0), ("gu", 1), ("down", 0), ("down", 1))))
        t0 += tiles
    return out


def column_tiles(w):
    rows, cols = w.shape
    return w.reshape(rows // P, P, cols // P, P).transpose(2, 1, 0, 3).reshape(cols // P, P, rows)


def columns(v):
    return v.reshape(-1, P).T


def kernel(**inputs):
    import concourse.bacc as bacc
    from concourse.bass_utils import run_bass_kernel_spmd

    a = {k: np.asarray(v) for k, v in inputs.items()}
    tiles = {"w_in": column_tiles(a["w_in"][0]), "w_rnn_out": column_tiles(a["w_rnn_out"][0]),
             "w_attn_out": column_tiles(a["w_attn_out"][0]), "w_o": column_tiles(a["w_o"][0])}
    w2 = a["attn_w_in_2"][0]
    w2 = np.concatenate([w2, np.zeros((w2.shape[0], 17 * P - w2.shape[1]), w2.dtype)], 1)
    tiles["attn_in"] = column_tiles(w2)
    tiles["attn_out"] = column_tiles(a["attn_w_out_2"][0])
    tiles["conv_in"] = column_tiles(a["conv_w_in_2"][0])
    tiles["conv_out"] = column_tiles(a["conv_w_out_2"][0])
    for layer in range(2):
        tiles[f"gate{layer}"] = column_tiles(a["ffn_w_gate_2"][layer])
        tiles[f"up{layer}"] = column_tiles(a["ffn_w_up_2"][layer])
        down = a["ffn_w_down_2"][layer]
        down = np.concatenate([down, np.zeros((3 * KC * P - down.shape[0], down.shape[1]), down.dtype)], 0)
        for g in range(3):
            tiles[f"down{layer}", g] = column_tiles(down[g * KC * P:(g + 1) * KC * P])
    stream = np.stack([tiles[t[0]][t[1]] if len(t) == 2 else tiles[t[0], t[2]][t[1]] for t in stream_plan()])
    assert len(stream) == T_END
    ada = a["ada_w_2"].reshape(2, KC, P, ADA_RANGES, ADA_W).transpose(0, 3, 1, 2, 4).reshape(-1, P, ADA_W)
    ada = np.concatenate([ada, np.zeros((4, P, ADA_W), ada.dtype)], 0)
    lru = np.concatenate([a["lru_w_a"][0], a["lru_w_x"][0]], 0).transpose(1, 0, 2).reshape(P, -1)
    prm = np.zeros((P, PRM_COLS), np.float32)

    def put(name, cols):
        at, n = PRM[name]
        prm[:, at:at + n] = cols

    put("norm_g", columns(a["norm_g"][0]))
    put("final_g", columns(a["final_norm_g"]))
    put("conv_w", np.concatenate([columns(a["conv_w"][0, j]) for j in range(4)], 1))
    put("conv_b", columns(a["conv_b"][0]))
    put("b_a", columns(a["lru_b_a"][0]))
    put("b_x", columns(a["lru_b_x"][0]))
    put("lam", columns(a["lru_lambda"][0]))
    put("sinks", np.broadcast_to(a["attn_sinks"][0], (P, 16)))
    put("norm1_g", columns(a["norm1_g_2"]))
    put("norm2_g", columns(a["norm2_g_2"]))
    put("ada_b", columns(a["ada_b_2"]))
    put("c", columns(a["c_2"][0]))
    put("q_g", np.tile(a["attn_q_norm_g_2"][0], 2)[:, None])
    put("k_g", np.tile(a["attn_k_norm_g_2"][0], 2)[:, None])
    put("ki_g", np.tile(a["idx_k_ln_g_2"][0], 2)[:, None])
    put("ki_b", np.tile(a["idx_k_ln_b_2"][0], 2)[:, None])
    put("conv3_w", np.concatenate([columns(a["conv_w_2"][0, j]) for j in range(3)], 1))
    pos = np.ascontiguousarray(np.broadcast_to(a["positions_2"].astype(np.int32), (P, S)))
    arrays = {
        "x_t": a["x"][0].T.reshape(KC, P, S).transpose(1, 0, 2).reshape(P, BIG),
        "weights": stream, "ada": ada, "lru_w": lru, "params": prm, "constants": constant_columns(),
        "rope1": first_rope_tables(), "positions": pos,
    }
    nc = bacc.Bacc("TRN2", target_bir_lowering=False, num_devices=1,
                   dynamic_dma_scratch_size=2048)
    args = []
    for name, arr in arrays.items():
        arrays[name] = arr = np.ascontiguousarray(arr)
        args.append(nc.dram_tensor(name, arr.shape, mybir.dt.from_np(arr.dtype), kind="ExternalInput").ap())
    args.append(nc.dram_tensor("y_t", (P, BIG), F32, kind="ExternalOutput").ap())
    build(nc, *args)
    got = run_bass_kernel_spmd(nc, [arrays], core_ids=[0]).results[0]["y_t"]
    return got.reshape(P, KC, S).transpose(2, 1, 0).reshape(1, S, KC * P)
```
